# Optimizing a Trainium2 kernel written in Bass

```python
import jax, jax.numpy as jnp
from jax import lax
import numpy as np

D_MODEL = 1024
BATCH = 1
SEQ = 512
DEPTH = 1
DEC_BATCH = 1
DEC_SEQ = 32
PAST_LEN = 256

CHUNK = 64
GMLP_CHUNK = 128
GMLP_GROUPS = 8
WIDTH_A = D_MODEL
GMLP_HEAD = WIDTH_A // GMLP_GROUPS
WIDTH_B = D_MODEL
CONV_WIDTH = 3
D_FF = ((8 * D_MODEL // 3 + 255) // 256) * 256
EPS = 1e-6
SPLITS = (WIDTH_A, WIDTH_A, WIDTH_B, WIDTH_B, WIDTH_B, D_MODEL, D_MODEL)
IN_COLS = sum(SPLITS)
SPLIT_IDX = tuple(int(i) for i in np.cumsum(SPLITS)[:-1])

kernel_name = "hybrid_gmlp_shortconv_streaming_step"

def rmsnorm(x, g):
    xf = x.astype(jnp.float32)
    r = lax.rsqrt(jnp.mean(xf * xf, axis=-1, keepdims=True) + EPS)
    return (xf * r).astype(x.dtype) * g

def layernorm(x, g, b):
    xf = x.astype(jnp.float32)
    mu = jnp.mean(xf, axis=-1, keepdims=True)
    var = jnp.mean(jnp.square(xf - mu), axis=-1, keepdims=True)
    return ((xf - mu) * lax.rsqrt(var + EPS)).astype(x.dtype) * g + b

def spatial_gate(v, w_s, b_s):
    bsz, L, _ = v.shape
    n_chunks = -(-L // GMLP_CHUNK)
    pad = n_chunks * GMLP_CHUNK - L
    vp = jnp.pad(v, ((0, 0), (0, pad), (0, 0)))
    vr = vp.reshape(bsz, n_chunks, GMLP_CHUNK, GMLP_GROUPS, GMLP_HEAD)
    mask = jnp.tril(jnp.ones((GMLP_CHUNK, GMLP_CHUNK), dtype=bool))
    ws = jnp.where(mask[None], w_s, jnp.zeros_like(w_s))
    out = jnp.einsum('gij,bcjgd->bcigd', ws, vr) + b_s.T[None, None, :, :, None]
    return out.reshape(bsz, n_chunks * GMLP_CHUNK, WIDTH_A)[:, :L]

def mixer(xn, conv_prev, w_in, ln_g, ln_b, w_s, b_s, conv_w, w_pa, w_pb, w_o):
    z = xn @ w_in
    u_a, v_a, bg, cg, hh, ga, gb = jnp.split(z, SPLIT_IDX, axis=-1)
    u = jax.nn.gelu(u_a, approximate=False)
    v = layernorm(jax.nn.gelu(v_a, approximate=False), ln_g, ln_b)
    a = u * spatial_gate(v, w_s, b_s)
    L = xn.shape[1]
    xc = jnp.concatenate([conv_prev, cg * hh], axis=1)
    conv = conv_w[0] * xc[:, :L] + conv_w[1] * xc[:, 1:L + 1] + conv_w[2] * xc[:, 2:]
    bconv = bg * conv
    m = jax.nn.sigmoid(ga) * (a @ w_pa) + jax.nn.sigmoid(gb) * (bconv @ w_pb)
    return m @ w_o, xc[:, -(CONV_WIDTH - 1):], v

def swiglu(x, w_gate, w_up, w_down):
    return (jax.nn.silu(x @ w_gate) * (x @ w_up)) @ w_down

def trunk(x, conv_states, norm_mix, w_in, ln_g, ln_b, w_s, b_s, conv_w,
          w_pa, w_pb, w_o, norm_ffn, w_gate, w_up, w_down, norm_final):
    new_conv, new_v = [], []
    for l in range(DEPTH):
        mo, c_new, v_rows = mixer(rmsnorm(x, norm_mix[l]), conv_states[l], w_in[l], ln_g[l], ln_b[l],
                                  w_s[l], b_s[l], conv_w[l], w_pa[l], w_pb[l], w_o[l])
        x = x + mo
        x = x + swiglu(rmsnorm(x, norm_ffn[l]), w_gate[l], w_up[l], w_down[l])
        new_conv.append(c_new)
        new_v.append(v_rows)
    return rmsnorm(x, norm_final), jnp.stack(new_conv), jnp.stack(new_v)

def setup_inputs(seed: int = 0) -> dict:
    key = jax.random.key(seed)
    ks = jax.random.split(key, 20)
    f32 = jnp.float32
    def nrm(k, shape, scale):
        return jax.random.normal(k, shape, f32) * scale
    return {
        "x_prompt": nrm(ks[0], (BATCH, SEQ, D_MODEL), 1.0),
        "x_sample": nrm(ks[1], (DEC_BATCH, DEC_SEQ, D_MODEL), 1.0),
        "state_conv": nrm(ks[2], (DEPTH, DEC_BATCH, CONV_WIDTH - 1, WIDTH_B), 1.0),
        "norm_mix": 1.0 + nrm(ks[3], (DEPTH, D_MODEL), 0.02),
        "w_in": nrm(ks[4], (DEPTH, D_MODEL, IN_COLS), D_MODEL ** -0.5),
        "gmlp_ln_g": 1.0 + nrm(ks[5], (DEPTH, WIDTH_A), 0.02),
        "gmlp_ln_b": nrm(ks[6], (DEPTH, WIDTH_A), 0.02),
        "w_s": nrm(ks[7], (DEPTH, GMLP_GROUPS, GMLP_CHUNK, GMLP_CHUNK), GMLP_CHUNK ** -0.5),
        "b_s": 1.0 + nrm(ks[8], (DEPTH, GMLP_GROUPS, GMLP_CHUNK), 0.02),
        "conv_w": nrm(ks[9], (DEPTH, CONV_WIDTH, WIDTH_B), CONV_WIDTH ** -0.5),
        "w_pa": nrm(ks[10], (DEPTH, WIDTH_A, D_MODEL), WIDTH_A ** -0.5),
        "w_pb": nrm(ks[11], (DEPTH, WIDTH_B, D_MODEL), WIDTH_B ** -0.5),
        "w_o": nrm(ks[12], (DEPTH, D_MODEL, D_MODEL), 0.5 * D_MODEL ** -0.5),
        "norm_ffn": 1.0 + nrm(ks[13], (DEPTH, D_MODEL), 0.02),
        "w_gate": nrm(ks[14], (DEPTH, D_MODEL, D_FF), D_MODEL ** -0.5),
        "w_up": nrm(ks[15], (DEPTH, D_MODEL, D_FF), D_MODEL ** -0.5),
        "w_down": nrm(ks[16], (DEPTH, D_FF, D_MODEL), 0.5 * D_FF ** -0.5),
        "norm_final": 1.0 + nrm(ks[17], (D_MODEL,), 0.02),
    }

def reference(x_prompt, x_sample, state_conv, norm_mix, w_in, gmlp_ln_g, gmlp_ln_b, w_s, b_s,
              conv_w, w_pa, w_pb, w_o, norm_ffn, w_gate, w_up, w_down, norm_final):
    params = (norm_mix, w_in, gmlp_ln_g, gmlp_ln_b, w_s, b_s, conv_w,
              w_pa, w_pb, w_o, norm_ffn, w_gate, w_up, w_down, norm_final)
    zero_conv = jnp.zeros((DEPTH, x_prompt.shape[0], CONV_WIDTH - 1, WIDTH_B), dtype=x_prompt.dtype)
    y_prompt, new_conv_prompt, _ = trunk(x_prompt, zero_conv, *params)
    y_sample, new_conv_sample, new_gmlp_v_sample = trunk(x_sample, state_conv, *params)
    return (y_prompt, y_sample, new_conv_prompt, new_conv_sample, new_gmlp_v_sample)


_drawn_inputs = setup_inputs


def setup_inputs(seed=0):
    import zlib

    import numpy as np

    out = dict(_drawn_inputs(seed))
    spreads = {}
    factors = {'gmlp_ln_g': 20.011,
     'gmlp_ln_b': 20.207,
     'b_s': 21.651,
     'norm_ffn': 6.997,
     'norm_final': 23.437,
     'state_conv': 3.262}
    for name, (base, spread) in spreads.items():
        noise = np.random.default_rng([zlib.crc32(name.encode()), seed]).standard_normal(out[name].shape)
        drawn = base * np.exp(spread * noise) if base else spread * noise
        out[name] = __import__('jax').numpy.asarray(drawn.astype(out[name].dtype))
    for name, factor in factors.items():
        out[name] = (out[name] * factor).astype(out[name].dtype)
    return out
```

```python
from contextlib import ExitStack

import concourse.bass as bass
from concourse import mybir

F32 = mybir.dt.float32
F32R = mybir.dt.float32r
ALU = mybir.AluOpType
ACT = mybir.ActivationFunctionType

P = 128
EPS = 1e-6

PHASES = {
    "v": (1, 4, 2, "aaaa"),
    "mix": (4, 4, 2, "adda"),
    "merge_a": (4, 2, 2, "ad"),
    "merge_b": (4, 2, 2, "ad"),
    "out": (2, 2, 2, "dd"),
    "ffn_1": (6, 2, 2, "dd"),
    "down_1": (4, 2, 1, "dd"),
    "ffn_2": (5, 2, 2, "dd"),
    "down_2": (4, 2, 1, "dd"),
}


class Phase:

    def __init__(self, name, unit0, tile0, freed):
        self.name = name
        self.iters, self.units, self.per_unit, self.by = PHASES[name]
        self.unit0, self.tile0 = unit0, tile0
        self.freed = freed

    def in_iter(self, engine, pair, units):
        return sum(2 for s in range(units)
                   if self.by[s] == engine and (self.per_unit == 2 or s % 2 == pair))

    def unit(self, j, s):
        return self.unit0 + s + self.units * j

    def loads(self, j, s):
        return (self.unit0 + s) // 2 + 1 + self.units // 2 * j

    def tile(self, j, s, i=0):
        return self.tile0 + s * self.per_unit + i + self.units * self.per_unit * j

    def pair(self, s, i):
        return i if self.per_unit == 2 else s % 2

    def out_before(self, engine, j, s, i=0):
        p = self.pair(s, i)
        return (self.freed[engine, p] + self.in_iter(engine, p, s)
                + self.in_iter(engine, p, self.units) * j)


    def takers(self, s):
        if self.per_unit == 2 and s > 0:
            return {self.by[s - 1]}
        return {self.by[-1], self.prev}


def make_phases():
    unit, tile = 0, 0
    freed = {(e, p): 0 for e in "ad" for p in range(2)}
    made, prev = {}, "a"
    for name in PHASES:
        ph = made[name] = Phase(name, unit, tile, dict(freed))
        ph.prev = prev
        prev = ph.by[-1]
        unit += ph.iters * ph.units
        tile += ph.iters * ph.units * ph.per_unit
        for e, p in freed:
            freed[e, p] += ph.in_iter(e, p, ph.units) * ph.iters
    return made, unit


def trunk_kernel(nc, x_prompt, x_sample, state_conv, norm_mix, w_in, ln_g, ln_b, w_s, b_s, conv_w,
                 w_pa, w_pb, w_o, norm_ffn, w_gate, w_up, w_down, norm_final,
                 y_prompt, y_sample, conv_prompt, conv_sample, v_sample):
    D = w_in.shape[1]
    NP, NS = x_prompt.shape[1], x_sample.shape[1]
    N = NP + NS
    HALF = N // 2
    KD = D // P
    NF = w_gate.shape[2] // P
    NF1 = 2 * PHASES["ffn_1"][0]
    NF2 = NF - NF1
    CH = NP // P
    ROWS = [P] * CH + [NS]
    UNIT = KD * 2 * P
    XC = N + 4
    CV = XC - 2
    H1P = NP - HALF
    ph, UNITS = make_phases()

    ctx = ExitStack()
    with ctx:
        start = (nc.sbuf_base + 63) // 64 * 64
        place = [start]

        def sb(name, shape, dt=F32, at=None):
            size = 4
            for n in shape[1:]:
                size *= n
            off = place[0] if at is None else at
            t = nc.alloc_sbuf_tensor_at(name, shape, dt, offset=off)
            if at is None:
                place[0] = off + (size + 31) // 32 * 32
            return t, off

        w_raw, _ = sb("w_raw", [P, 2, UNIT])
        w_hi, _ = sb("w_hi", [P, 2, UNIT], F32R)
        w_lo, _ = sb("w_lo", [P, 2, UNIT], F32R)
        act_hi, hi_at = sb("act_hi", [P, 3 * KD, N], F32R)
        act_lo, lo_at = sb("act_lo", [P, 3 * KD, N], F32R)
        XN, A0, B0, M0, H0 = 0, KD, 2 * KD, KD, KD
        resid, resid_at = sb("resid", [P, KD, N])
        tok, tok_at = sb("tok", [P, CH + 1, D])
        wsbs, wsbs_at = sb("wsbs", [P, 2, D])
        mixbuf, mixbuf_at = sb("mixbuf", [P, XC + 4 + (CH + 1) * P + P])
        ident, _ = sb("ident", [P, P])
        ones, _ = sb("ones", [P, P])
        rows48, _ = sb("rows48", [6 * KD, P])
        cols48, _ = sb("cols48", [P, 6 * KD])
        states, _ = sb("states", [P, 4, KD])
        states_out, _ = sb("states_out", [4 * KD, P])
        stats, _ = sb("stats", [P, CH + 1, 2, 6])
        meanvar, _ = sb("meanvar", [P, CH + 1, 2])
        sumsq, _ = sb("sumsq", [P, CH + 1])
        sumsq_m, _ = sb("sumsq_m", [P, CH + 1, KD])
        msq, _ = sb("msq", [P, CH + 1])
        root, _ = sb("root", [P, CH + 1])
        rstd, _ = sb("rstd", [P, CH + 1])
        newton, _ = sb("newton", [P, CH + 1])
        assert place[0] <= nc.sbuf_usable_end

        g1_all, _ = sb("g1_all", [P, D], at=hi_at + A0 * N * 4)
        lng_all, _ = sb("lng_all", [P, D], at=hi_at + A0 * N * 4 + 4 * D)
        lnb_all, _ = sb("lnb_all", [P, D], at=hi_at + A0 * N * 4 + 8 * D)
        ws_in, _ = sb("ws_in", [P, KD, P], at=hi_at + A0 * N * 4 + 12 * D)
        x_scaled, _ = sb("x_scaled", [P, 2, D], at=lo_at + A0 * N * 4)
        junk, _ = sb("junk", [P, D], at=lo_at + A0 * N * 4 + 8 * D)
        gelu_v, _ = sb("gelu_v", [P, 2, N], at=lo_at + A0 * N * 4 + 12 * D)
        gf_all, _ = sb("gf_all", [P, D], at=hi_at + (A0 + NF1) * N * 4)
        junk_y, _ = sb("junk_y", [P, CH + 1, P], at=lo_at + (A0 + NF1) * N * 4)
        c_sb, _ = sb("c_sb", [P, 2, N], at=resid_at)
        u_sb, _ = sb("u_sb", [P, 2, N], at=resid_at + 8 * N)
        prod, _ = sb("prod", [P, N], at=resid_at + 16 * N)
        conv, _ = sb("conv", [P, 2, CV], at=resid_at + 20 * N)
        assert 20 * N + 8 * CV <= KD * N * 4
        m_a, _ = sb("m_a", [P, KD, N], at=tok_at)
        sq_sum, _ = sb("sq_sum", [P, N], at=tok_at)
        sq_one, _ = sb("sq_one", [P, N], at=tok_at + 4 * N)
        r_all, _ = sb("r_all", [P, N], at=tok_at + 8 * N)
        gate_sb, _ = sb("gate_sb", [P, 2, N], at=tok_at + 12 * N)
        up_sb, _ = sb("up_sb", [P, N], at=tok_at + 20 * N)
        r_diag, _ = sb("r_diag", [P, CH + 1, P], at=tok_at + 24 * N)
        ws_t, _ = sb("ws_t", [P, KD, P], at=wsbs_at)
        bs_all, _ = sb("bs_all", [P, KD, P], at=wsbs_at + 4 * D)
        x_again, _ = sb("x_again", [P, D], at=wsbs_at)
        xc, _ = sb("xc", [P, XC], at=mixbuf_at)
        v_stage, _ = sb("v_stage", [P, CH + 1, P], at=mixbuf_at + 4 * (XC + 4))
        ws_stage, _ = sb("ws_stage", [P, P], at=mixbuf_at + 4 * (XC + 4 + (CH + 1) * P))
        sig, _ = sb("sig", [P, 2, N], at=mixbuf_at)
        x_last, _ = sb("x_last", [P, 2, N], at=mixbuf_at)

        ps_main = ctx.enter_context(nc.psum_tensor("ps_main", [P, 2, 2, 512], F32))
        ps_t = ctx.enter_context(nc.psum_tensor("ps_t", [P, 2, 512], F32))
        ps_g = ctx.enter_context(nc.psum_tensor("ps_g", [P, 2, 512], F32))
        ps_misc = [ps_t, ps_g]
        ps_blocks = [t[:].rearrange("p b (m n) -> p (b m) n", n=P) for t in ps_misc]

        def sem(name):
            return ctx.enter_context(nc.semaphore(name))

        raw_loaded = [sem(f"raw_loaded{n}") for n in range(2)]
        first_loaded = sem("first_loaded")
        x_loaded = [sem(f"x_loaded{c}") for c in range(CH + 1)]
        g1_loaded = sem("g1_loaded")
        rows_loaded = sem("rows_loaded")
        ws_loaded = sem("ws_loaded")
        bs_loaded = sem("bs_loaded")
        ln_loaded = sem("ln_loaded")
        again_loaded = sem("again_loaded")
        gf_loaded = sem("gf_loaded")
        stored = sem("stored")
        v_stored = sem("v_stored")

        hi_ready = sem("hi_ready")
        lo_ready = sem("lo_ready")
        first_hi = sem("first_hi")
        first_lo = sem("first_lo")
        tile_half = sem("tile_half")
        act_out = [sem(f"act_out{p}") for p in range(2)]
        dve_out = [sem(f"dve_out{p}") for p in range(2)]

        zero_set = sem("zero_set")
        stats_set = sem("stats_set")
        consts_ready = sem("consts_ready")
        pads_ready = sem("pads_ready")
        rows_turned = sem("rows_turned")
        cols_ready = sem("cols_ready")
        ws_turned = sem("ws_turned")
        ws_copied = sem("ws_copied")
        ws_ready = sem("ws_ready")
        squares_done = sem("squares_done")
        msq_done = sem("msq_done")
        root_done = sem("root_done")
        xs_ready = sem("xs_ready")
        xs_turned = sem("xs_turned")
        xn_hi = sem("xn_hi")
        xn_ready = sem("xn_ready")
        v_turned = sem("v_turned")
        v_in_tok = sem("v_in_tok")
        stats_done = sem("stats_done")
        v_centred = sem("v_centred")
        v_step = sem("v_step")
        v_ready = sem("v_ready")
        staged_half = sem("staged_half")
        staged = sem("staged")
        gated = sem("gated")
        gate_out = sem("gate_out")
        b_ready = sem("b_ready")
        a_ready = sem("a_ready")
        states_copied = sem("states_copied")
        states_turned = sem("states_turned")
        states_ready = sem("states_ready")
        x_turned = sem("x_turned")
        resid_ready = sem("resid_ready")
        m_ready = sem("m_ready")
        xg_ready = sem("xg_ready")
        sq_done = sem("sq_done")
        sum_done = sem("sum_done")
        sums_turned = sem("sums_turned")
        diag_ready = sem("diag_ready")
        r_turned = sem("r_turned")
        r_ready = sem("r_ready")
        silu_done = sem("silu_done")
        h_ready = sem("h_ready")
        y_turned = sem("y_turned")
        y_in_tok = sem("y_in_tok")
        ysq_done = sem("ysq_done")
        ysum_done = sem("ysum_done")
        y_ready = sem("y_ready")
        dve_step = sem("dve_step")

        def halves(ap):
            return ap.rearrange("p (h n) -> p h n", h=2)

        def wait(eng, s, n):
            if not isinstance(n, int) or n > 0:
                eng.wait_ge(s, n)

        def fbits(ap):
            return ap.bitcast(F32)

        block = ctx.enter_context(nc.Block())

        @block.sync
        def _(sp):
            def row_blocks(w, rows, n, width):
                return w[0, rows, bass.ds(width * n, width)].rearrange("(k p) n -> p k n", p=P)

            def slot_free(p, j, s):
                sp.wait_ge(raw_loaded[s % 2], 16)
                sp.wait_ge(lo_ready, p.unit(j, s) - 2)

            def load(p, j, s, w, n):
                slot_free(p, j, s)
                dst = w_raw[:, s % 2, :].rearrange("p (k n) -> p k n", k=KD)
                sp.dma_start(dst, row_blocks(w, slice(0, D), n, 2 * P)).then_inc(raw_loaded[s % 2], 16)

            def load_down(p, j, s, row, blocks):
                slot_free(p, j, s)
                dst = w_raw[:, s % 2, 0:blocks * P].rearrange("p (k n) -> p k n", k=blocks)
                src = row_blocks(w_down, slice(row, row + blocks * P), 2 * j + s, P)
                sp.dma_start(dst, src).then_inc(raw_loaded[s % 2], 16)

            def x_rows(c):
                return x_prompt[0, c * P:(c + 1) * P, :] if c < CH else x_sample[0]

            def load_x(c):
                sp.dma_start(tok[0:ROWS[c], c, :], x_rows(c)).then_inc(x_loaded[c], 16)

            V0, BG, CG, HH, GA, GB = (n * D // (2 * P) for n in range(1, 7))
            load_x(0)
            sp.dma_start(g1_all[:], norm_mix[0:1, :].to_broadcast((P, D))).then_inc(g1_loaded, 16)
            load_x(1)
            load_x(2)
            for n, done in ((0, raw_loaded[0]), (1, first_loaded)):
                dst = w_raw[:, 0, n * UNIT // 2:(n + 1) * UNIT // 2].rearrange("p (k n) -> p k n", k=KD // 2)
                sp.dma_start(dst, row_blocks(w_in, slice(n * D // 2, (n + 1) * D // 2), V0, 2 * P)).then_inc(done, 16)
            load_x(3)
            load_x(4)
            pv = ph["v"]
            dst = w_raw[:, 1, :].rearrange("p (k n) -> p k n", k=KD)
            sp.dma_start(dst, row_blocks(w_in, slice(0, D), V0 + 1, 2 * P)).then_inc(raw_loaded[1], 16)
            r = 0
            for src, n in ((state_conv[0, 0].rearrange("w (m c) -> (w m) c", c=P), 2 * KD),
                           (conv_w[0].rearrange("w (m c) -> (w m) c", c=P), 3 * KD),
                           (norm_ffn[0].rearrange("(m c) -> m c", c=P), KD)):
                sp.dma_start(rows48[r:r + n, :], src).then_inc(rows_loaded, 16)
                r += n
            sp.dma_start(ws_in[:], w_s[0].rearrange("g i j -> i g j")).then_inc(ws_loaded, 16)
            sp.dma_start(bs_all[:].rearrange("p g i -> p (g i)"),
                         b_s.rearrange("a g i -> a (g i)").to_broadcast((P, D))).then_inc(bs_loaded, 16)
            sp.dma_start(lng_all[:], ln_g[0:1, :].to_broadcast((P, D))).then_inc(ln_loaded, 16)
            sp.dma_start(lnb_all[:], ln_b[0:1, :].to_broadcast((P, D))).then_inc(ln_loaded, 16)
            sp.wait_ge(first_lo, 2)
            sp.dma_start(w_raw[:, 0, :].rearrange("p (k n) -> p k n", k=KD),
                         row_blocks(w_in, slice(0, D), V0 + 2, 2 * P)).then_inc(raw_loaded[0], 16)
            load(pv, 0, 3, w_in, V0 + 3)
            with sp.Fori(0, 4) as j:
                for s, part in enumerate((CG, HH, BG, 0)):
                    load(ph["mix"], j, s, w_in, j + part)
            sp.wait_ge(v_ready, CH + 1)
            sp.dma_start(v_sample[0, 0], tok[0:NS, CH, :]).then_inc(v_stored, 16)
            with sp.Fori(0, 4) as j:
                load(ph["merge_a"], j, 0, w_in, j + GA)
                load(ph["merge_a"], j, 1, w_pa, j)
            sp.wait_ge(states_ready, 1)
            sp.dma_start(conv_prompt[0, 0].rearrange("w (m c) -> (w m) c", c=P),
                         states_out[0:2 * KD, :]).then_inc(stored, 16)
            sp.dma_start(conv_sample[0, 0].rearrange("w (m c) -> (w m) c", c=P),
                         states_out[2 * KD:4 * KD, :]).then_inc(stored, 16)
            with sp.Fori(0, 4) as j:
                load(ph["merge_b"], j, 0, w_in, j + GB)
                load(ph["merge_b"], j, 1, w_pb, j)
            with sp.Fori(0, 2) as j:
                for s in range(2):
                    load(ph["out"], j, s, w_o, 2 * j + s)
            with sp.Fori(0, NF1 // 2) as j:
                load(ph["ffn_1"], j, 0, w_gate, j)
                load(ph["ffn_1"], j, 1, w_up, j)
            with sp.Fori(0, 4) as j:
                for s in range(2):
                    load_down(ph["down_1"], j, s, 0, NF1)
            sp.dma_start(gf_all[:], norm_final.rearrange("(a d) -> a d", a=1).to_broadcast((P, D))).then_inc(gf_loaded, 16)
            with sp.Fori(0, NF2 // 2) as j:
                load(ph["ffn_2"], j, 0, w_gate, j + NF1 // 2)
                load(ph["ffn_2"], j, 1, w_up, j + NF1 // 2)
            with sp.Fori(0, 4) as j:
                for s in range(2):
                    load_down(ph["down_2"], j, s, NF1 * P, NF2)
            for c in range(CH + 1):
                sp.wait_ge(y_ready, c + 1)
                dst = y_prompt[0, c * P:(c + 1) * P, :] if c < CH else y_sample[0]
                sp.dma_start(dst, tok[0:ROWS[c], c, :]).then_inc(stored, 16)
            sp.wait_ge(v_stored, 16)
            sp.wait_ge(stored, 16 * (2 + CH + 1))

        @block.tensor
        def _(pe):
            def product_half(p, j, s, i, h, blocks, x0, width, ready=None):
                pair = p.pair(s, i)
                out = ps_main[:, pair, h, 0:HALF]
                tok_h = slice(h * HALF, (h + 1) * HALF)
                for k in range(blocks):
                    if ready is not None:
                        ready(k, h)
                    at = k * width + (i * P if p.per_unit == 2 else 0)
                    whi = w_hi[:, s % 2, at:at + P]
                    wlo = w_lo[:, s % 2, at:at + P]
                    xhi, xlo = act_hi[:, x0 + k, tok_h], act_lo[:, x0 + k, tok_h]
                    pe.matmul(out, whi, xhi, start=(k == 0), stop=False)
                    pe.matmul(out, whi, xlo, start=False, stop=False)
                    last = pe.matmul(out, wlo, xhi, start=False, stop=(k == blocks - 1))
                last.then_inc(tile_half, 1)

            def pair_free(p, j, s, i):
                pair = p.pair(s, i)
                if p.name == "v" and s == 0:
                    return
                if "a" in p.takers(s):
                    pe.wait_ge(act_out[pair], p.out_before("a", j, s, i))
                if "d" in p.takers(s):
                    pe.wait_ge(dve_out[pair], p.out_before("d", j, s, i))

            def unit(p, j, s, x0, blocks=KD, ready=None, between=None):
                pe.wait_ge(lo_ready, p.unit(j, s))
                for i in range(p.per_unit):
                    pair_free(p, j, s, i)
                    for h in range(2):
                        product_half(p, j, s, i, h, blocks, x0, 2 * P if p.per_unit == 2 else P,
                                     ready if i == 0 and s == 0 else None)
                    if between is not None:
                        between(i)

            def turn_blocks(out, src, rows):
                for m in range(KD):
                    last = pe.transpose(out[:, m, 0:rows], src[0:rows, m * P:(m + 1) * P], ident[0:rows, 0:rows])
                return last

            def turn_tokens(out, src):
                for c in range(CH + 1):
                    dst = out[0:P, 0, c * P:(c + 1) * P] if c < CH else out[0:NS, 1, 0:P]
                    last = pe.transpose(dst, src[:, c * P:c * P + ROWS[c]], ident[:, :])
                return last

            def turn_x(c):
                pe.wait_ge(xs_ready, c + 1)
                if c >= 2:
                    pe.wait_ge(xn_ready, c - 1)
                turn_blocks(ps_blocks[c % 2], x_scaled[:, c % 2, :], ROWS[c]).then_inc(xs_turned, 1)

            pe.wait_ge(consts_ready, 2)
            for c in range(3):
                turn_x(c)

            pv = ph["v"]
            pe.wait_ge(xn_ready, 3)

            def first_rows(k, h):
                if h == 0 and k % (KD // 2) == 0:
                    pe.wait_ge(first_lo, k // (KD // 2) + 1)
            product_half(pv, 0, 0, 0, 0, KD, XN, 2 * P, first_rows)
            for c in range(3, CH + 1):
                turn_x(c)
            pe.wait_ge(xn_ready, CH + 1)
            product_half(pv, 0, 0, 0, 1, KD, XN, 2 * P)

            def turn_v(t):
                pe.wait_ge(act_out[t % 2], 2 * (t // 2 + 1))
                if t >= 1:
                    pe.wait_ge(v_in_tok, t)
                turn_tokens(ps_t, gelu_v[:, t % 2, :]).then_inc(v_turned, 1)

            for t in range(1, 2 * pv.units):
                s, i = divmod(t, 2)
                if i == 0:
                    pe.wait_ge(lo_ready, s)
                pair_free(pv, 0, s, i)
                for h in range(2):
                    product_half(pv, 0, s, i, h, KD, XN, 2 * P)
                turn_v(t - 1)
                if t == 1:
                    pe.wait_ge(rows_loaded, 48)
                    pe.transpose(ps_g[:, 0, 0:6 * KD], rows48[:, :], ident[0:6 * KD, 0:6 * KD]).then_inc(rows_turned, 1)
                if t == 2:
                    pe.wait_ge(cols_ready, 1)
                    pe.wait_ge(ws_loaded, 16)
                    for g in range(KD):
                        last = pe.transpose(ps_blocks[1][:, g, :], ws_in[:, g, :], ident[:, :])
                    last.then_inc(ws_turned, 1)
            turn_v(2 * pv.units - 1)

            with pe.Fori(0, 4) as j:
                p = ph["mix"]

                def mix_positions(i):
                    g = 2 * j + i
                    pe.wait_ge(staged, g + 1)
                    if i == 1:
                        pe.wait_ge(gate_out, g)
                    for c in range(CH):
                        pe.matmul(ps_g[:, 0, c * P:(c + 1) * P], v_stage[:, c, :], ws_stage[:, :], start=True, stop=True)
                    pe.matmul(ps_g[:, 1, 0:NS], v_stage[0:NS, CH, :], ws_stage[0:NS, 0:NS],
                              start=True, stop=True).then_inc(gated, 1)

                for s in range(3):
                    unit(p, j, s, XN)
                mix_positions(0)
                unit(p, j, 3, XN, between=lambda i: mix_positions(1) if i == 0 else None)

            pe.wait_ge(states_copied, KD)
            pe.transpose(ps_t[0:4 * KD, 0, 0:P], states[:].rearrange("p w m -> p (w m)"), ident[:, :]).then_inc(states_turned, 1)

            with pe.Fori(0, 4) as j:
                p = ph["merge_a"]
                unit(p, j, 0, XN)
                pe.wait_ge(again_loaded, 16 * j + 16)
                pe.wait_ge(act_out[0], p.out_before("a", j, 1, 0))
                turn_blocks(ps_blocks[1], x_again, P).then_inc(x_turned, 1)
                pe.wait_ge(a_ready, KD)
                unit(p, j, 1, A0)
            pe.wait_ge(again_loaded, 16 * (CH + 1))
            pe.wait_ge(resid_ready, CH)
            turn_blocks(ps_blocks[1], x_again, NS).then_inc(x_turned, 1)
            with pe.Fori(0, 4) as j:
                p = ph["merge_b"]
                unit(p, j, 0, XN)
                pe.wait_ge(b_ready, KD)
                unit(p, j, 1, B0)
            with pe.Fori(0, 2) as j:
                p = ph["out"]
                for s in range(2):
                    unit(p, j, s, M0, ready=lambda k, h: pe.wait_ge(m_ready, 2 * k + h + 1))

            def xg_there(k, h):
                pe.wait_ge(xg_ready, 2 * k + h + 1)

            p = ph["ffn_1"]

            def norm_sums(i):
                if i == 0:
                    pe.wait_ge(sum_done, KD + 1)
                    for c in range(CH + 1):
                        last = pe.matmul(ps_t[0:ROWS[c], 0, c:c + 1], sq_sum[:, c * P:c * P + ROWS[c]],
                                         ones[:, 0:1], start=True, stop=True)
                    last.then_inc(sums_turned, 1)
                else:
                    pe.wait_ge(diag_ready, CH + 1)
                    for c in range(CH + 1):
                        n = ROWS[c]
                        dst = ps_g[:, 0, c * P:(c + 1) * P] if c < CH else ps_g[:, 1, 0:NS]
                        last = pe.matmul(dst, ones[0:n, :], r_diag[0:n, c, 0:n], start=True, stop=True)
                    last.then_inc(r_turned, 1)

            unit(p, 0, 0, XN, ready=xg_there, between=norm_sums)
            unit(p, 0, 1, XN)
            with pe.Fori(1, NF1 // 2) as j:
                unit(p, j, 0, XN)
                unit(p, j, 1, XN)
            with pe.Fori(0, 4) as j:
                for s in range(2):
                    unit(ph["down_1"], j, s, H0, NF1, ready=lambda k, h: pe.wait_ge(h_ready, 2 * k + h + 1))
            with pe.Fori(0, NF2 // 2) as j:
                unit(ph["ffn_2"], j, 0, XN)
                unit(ph["ffn_2"], j, 1, XN)

            p = ph["down_2"]

            def down(j, s):
                unit(p, j, s, H0, NF2, ready=lambda k, h: pe.wait_ge(h_ready, 2 * NF1 + 2 * k + h + 1))

            def turn_y(j, s):
                pe.wait_ge(dve_out[s], p.out_before("d", j, s) + 2)
                turn_tokens(ps_misc[s], x_last[:, s, :]).then_inc(y_turned, 1)

            down(0, 0)
            with pe.Fori(0, 3) as j:
                down(j, 1)
                turn_y(j, 0)
                down(j + 1, 0)
                turn_y(j, 1)
            down(3, 1)
            turn_y(3, 0)
            turn_y(3, 1)

        @block.scalar
        def _(act):
            def split_hi(p, j, s):
                slot = (s + 1) % 2
                act.wait_ge(raw_loaded[slot], 16 * p.loads(j, s + 1))
                wait(act, tile_half, 2 * p.tile(j, s))
                act.copy(w_hi[:, slot, :], w_raw[:, slot, :]).then_inc(hi_ready, 1)

            def take(p, j, s, i, out, func):
                pair = p.pair(s, i)
                act.wait_ge(tile_half, 2 * p.tile(j, s, i) + 2)
                act.activation(halves(out), ps_main[:, pair, :, 0:HALF], func).then_inc(act_out[pair], 2)

            act.wait_ge(stats_set, 4)

            def squares(c):
                act.wait_ge(x_loaded[c], 16)
                if c:
                    act.wait_ge(squares_done, c)
                n = ROWS[c]
                act.activation(junk[0:n, :], tok[0:n, c, :], ACT.Square,
                               accum_out=sumsq[0:n, c:c + 1]).then_inc(squares_done, 1)
                act.wait_ge(msq_done, c + 1)
                act.activation(root[0:n, c:c + 1], msq[0:n, c:c + 1], ACT.Sqrt).then_inc(root_done, 1)

            def take_xn(c):
                act.wait_ge(xs_turned, c + 1)
                act.copy(act_hi[:, XN:XN + KD, c * P:c * P + ROWS[c]],
                         ps_blocks[c % 2][:, :, 0:ROWS[c]]).then_inc(xn_hi, 1)

            squares(0)
            squares(1)
            take_xn(0)
            squares(2)
            take_xn(1)
            take_xn(2)
            squares(3)
            squares(4)
            take_xn(3)
            take_xn(4)

            p = ph["v"]
            for t in range(2 * p.units):
                s, i = divmod(t, 2)
                if i == 0:
                    split_hi(p, 0, s)
                if t >= 2:
                    act.wait_ge(v_turned, t - 1)
                take(p, 0, s, i, gelu_v[:, i, :], ACT.Gelu)
                if t == 1:
                    act.wait_ge(rows_turned, 1)
                    act.copy(cols48[:], ps_g[:, 0, 0:6 * KD]).then_inc(cols_ready, 1)
                if t == 2:
                    act.wait_ge(ws_turned, 1)
                    act.copy(ws_t[:], ps_blocks[1]).then_inc(ws_copied, 1)

            p = ph["mix"]

            def mix(j):
                split_hi(p, j, 0)
                for i in range(2):
                    if not isinstance(j, int):
                        act.wait_ge(dve_out[i], p.out_before("d", j, 0, i))
                    take(p, j, 0, i, c_sb[:, i, :], ACT.Copy)
                if isinstance(j, int):
                    act.wait_ge(msq_done, CH + 2)
                    act.activation(root[:], msq[:], ACT.Sqrt).then_inc(root_done, 1)
                split_hi(p, j, 1)
                split_hi(p, j, 2)
                split_hi(p, j, 3)
                for i in range(2):
                    act.wait_ge(dve_out[i], p.out_before("d", j, 3, i))
                    take(p, j, 3, i, u_sb[:, i, :], ACT.Gelu)

            mix(0)
            with act.Fori(1, 4) as j:
                mix(j)

            def sigmoids(p, j):
                split_hi(p, j, 0)
                for i in range(2):
                    act.wait_ge(dve_out[i], p.out_before("d", j, 0, i))
                    take(p, j, 0, i, sig[:, i, :], ACT.Sigmoid)

            p = ph["merge_a"]
            act.wait_ge(states_turned, 1)
            act.copy(states_out[:], ps_t[0:4 * KD, 0, 0:P]).then_inc(states_ready, 1)
            act.wait_ge(gated, KD)
            act.wait_ge(b_ready, KD)
            act.wait_ge(a_ready, KD)
            with act.Fori(0, 4) as j:
                sigmoids(p, j)
                act.wait_ge(x_turned, j + 1)
                act.copy(resid[:, :, bass.ds(P * j, P)], ps_blocks[1]).then_inc(resid_ready, 1)
                split_hi(p, j, 1)
            act.wait_ge(x_turned, CH + 1)
            act.copy(resid[:, :, NP:N], ps_blocks[1][:, :, 0:NS]).then_inc(resid_ready, 1)

            p = ph["merge_b"]
            sigmoids(p, 0)
            split_hi(p, 0, 1)
            with act.Fori(1, 4) as j:
                act.wait_ge(m_ready, 4 * j)
                sigmoids(p, j)
                split_hi(p, j, 1)

            with act.Fori(0, 2) as j:
                for s in range(2):
                    split_hi(ph["out"], j, s)

            def silus(p, j):
                for i in range(2):
                    act.wait_ge(dve_out[i], p.out_before("d", j, 0, i) + 2)
                    act.activation(gate_sb[:, i, :], gate_sb[:, i, :], ACT.Silu).then_inc(silu_done, 1)

            p = ph["ffn_1"]
            split_hi(p, 0, 0)
            act.wait_ge(msq_done, CH + 3)
            act.activation(root[:], msq[:], ACT.Sqrt).then_inc(root_done, 1)
            silus(p, 0)
            split_hi(p, 0, 1)
            with act.Fori(1, NF1 // 2) as j:
                split_hi(p, j, 0)
                silus(p, j)
                split_hi(p, j, 1)
            with act.Fori(0, 4) as j:
                split_hi(ph["down_1"], j, 0)
                split_hi(ph["down_1"], j, 1)
            p = ph["ffn_2"]
            with act.Fori(0, NF2 // 2) as j:
                split_hi(p, j, 0)
                silus(p, j)
                split_hi(p, j, 1)

            p = ph["down_2"]

            def y_squares(m):
                act.wait_ge(y_in_tok, m + 1)
                if not isinstance(m, int) or m:
                    act.wait_ge(ysq_done, m)
                for c in range(CH + 1):
                    n = ROWS[c]
                    last = act.activation(junk_y[0:n, c, :], tok[0:n, c, bass.ds(P * m, P)], ACT.Square,
                                          accum_out=sumsq_m[0:n, c, bass.ds(m, 1)])
                last.then_inc(ysq_done, 1)

            split_hi(p, 0, 0)
            split_hi(p, 0, 1)
            y_squares(0)
            split_hi(p, 1, 0)
            y_squares(1)
            with act.Fori(1, 3) as j:
                split_hi(p, j, 1)
                y_squares(2 * j)
                split_hi(p, j + 1, 0)
                y_squares(2 * j + 1)
            y_squares(KD - 2)
            y_squares(KD - 1)
            act.wait_ge(msq_done, CH + 4)
            act.activation(root[:], msq[:], ACT.Sqrt).then_inc(root_done, 1)

        @block.vector
        def _(dve):
            steps = [0]

            def link(ins):
                steps[0] += 1
                ins.then_inc(dve_step, 1)
                dve.wait_ge(dve_step, steps[0])

            def loop(j, first, before, count):
                steps[0] = before + count * (j - first)

            def inverse_root(norm, n=P, cols=slice(0, CH + 1)):
                x, r, t = msq[0:n, cols], rstd[0:n, cols], newton[0:n, cols]
                dve.wait_ge(root_done, norm)
                link(dve.reciprocal(r, root[0:n, cols]))
                link(dve.tensor_tensor(t, x, r, ALU.mult))
                link(dve.tensor_tensor(t, t, r, ALU.mult))
                link(dve.tensor_scalar(t, t, -0.5, 1.5, ALU.mult, ALU.add))
                link(dve.tensor_tensor(r, r, t, ALU.mult))

            def split_lo(p, j, s):
                slot = (s + 1) % 2
                dve.wait_ge(hi_ready, p.unit(j, s + 1))
                dve.tensor_tensor(w_lo[:, slot, :], w_raw[:, slot, :], fbits(w_hi[:, slot, :]),
                                  ALU.subtract).then_inc(lo_ready, 1)

            def psum_half(p, s, i, h, a=0, b=HALF):
                return ps_main[:, p.pair(s, i), h, a:b]

            def done(p, j, s, i, h=1):
                dve.wait_ge(tile_half, 2 * p.tile(j, s, i) + h + 1)

            def scale_x(c):
                n = ROWS[c]
                dve.wait_ge(squares_done, c + 1)
                dve.tensor_scalar(msq[0:n, c:c + 1], sumsq[0:n, c:c + 1], 1.0 / D, EPS,
                                  ALU.mult, ALU.add).then_inc(msq_done, 1)
                inverse_root(c + 1, n, slice(c, c + 1))
                if c == 0:
                    dve.wait_ge(g1_loaded, 16)
                if c >= 2:
                    dve.wait_ge(xs_turned, c - 1)
                dve.scalar_tensor_tensor(x_scaled[0:n, c % 2, :], tok[0:n, c, :], rstd[0:n, c:c + 1],
                                         g1_all[0:n, :], ALU.mult, ALU.mult).then_inc(xs_ready, 1)

            def take_xn(c):
                dve.wait_ge(xn_hi, c + 1)
                cols = slice(c * P, c * P + ROWS[c])
                dve.tensor_tensor(act_lo[:, XN:XN + KD, cols], ps_blocks[c % 2][:, :, 0:ROWS[c]],
                                  fbits(act_hi[:, XN:XN + KD, cols]), ALU.subtract).then_inc(xn_ready, 1)

            dve.wait_ge(stats_set, 4)
            scale_x(0)
            scale_x(1)
            take_xn(0)
            scale_x(2)
            take_xn(1)
            take_xn(2)
            scale_x(3)
            scale_x(4)
            take_xn(3)
            take_xn(4)

            p = ph["v"]

            def take_v(t):
                dve.wait_ge(v_turned, t + 1)
                dve.tensor_copy(tok[:, 0:CH, t * P:(t + 1) * P],
                                ps_t[:, 0, :].rearrange("p (c n) -> p c n", c=CH))
                dve.tensor_copy(tok[0:NS, CH, t * P:(t + 1) * P], ps_t[0:NS, 1, 0:P]).then_inc(v_in_tok, 1)

            def v_stats(part):
                dve.wait_ge(v_in_tok, KD // 2 * (part + 1))
                for c in range(CH + 1):
                    n = ROWS[c]
                    last = dve.bn_stats(stats[0:n, c, part, :], tok[0:n, c, part * D // 2:(part + 1) * D // 2])
                last.then_inc(stats_done, 1)

            for s in range(p.units):
                split_lo(p, 0, s)
                if s:
                    take_v(2 * s - 1)
                if s == 2:
                    v_stats(0)
                take_v(2 * s)
            take_v(KD - 1)
            mix = ph["mix"]
            split_lo(mix, 0, 0)
            v_stats(1)
            dve.wait_ge(stats_done, 2)
            for c in range(CH + 1):
                last = dve.bn_aggr(meanvar[0:ROWS[c], c, :], stats[0:ROWS[c], c, :, :])
            link(last)
            dve.tensor_scalar(msq[:], meanvar[:, :, 1], EPS, None, ALU.add).then_inc(msq_done, 1)
            inverse_root(CH + 2)
            for c in range(CH + 1):
                n = ROWS[c]
                dve.tensor_scalar(tok[0:n, c, :], tok[0:n, c, :], meanvar[0:n, c, 0:1], rstd[0:n, c:c + 1],
                                  ALU.subtract, ALU.mult).then_inc(v_centred, 1)

            p = mix

            def split_block(x, block, signal):
                link(dve.tensor_copy(act_hi[:, block, :], x))
                dve.tensor_tensor(act_lo[:, block, :], x, fbits(act_hi[:, block, :]), ALU.subtract).then_inc(signal, 1)

            def col(n, m):
                return cols48[:, bass.ds(n * KD + m, 1)]

            def convolve(j, i):
                m = 2 * j + i
                dve.tensor_copy(xc[:, NP + 2:NP + 4], cols48[:, 0:2 * KD].rearrange("p (w m) -> p w m", w=2)[:, :, m])
                done(p, j, 1, i)
                dve.wait_ge(act_out[i], p.out_before("a", j, 1, i))
                c = c_sb[:, i, :]
                dve.tensor_tensor(xc[:, 2:2 + HALF], c[:, 0:HALF], psum_half(p, 1, i, 0), ALU.mult)
                dve.tensor_tensor(xc[:, 2 + HALF:2 + NP], c[:, HALF:NP], psum_half(p, 1, i, 1, 0, H1P), ALU.mult)
                dve.tensor_tensor(xc[:, NP + 4:N + 4], c[:, NP:N], psum_half(p, 1, i, 1, H1P),
                                  ALU.mult).then_inc(dve_out[i], 2)
                dve.wait_ge(dve_out[i], p.out_before("d", j, 2, i))
                dve.tensor_copy(states[:, 0:2, m], xc[:, NP:NP + 2])
                dve.tensor_copy(states[:, 2:4, m], xc[:, N + 2:N + 4]).then_inc(states_copied, 1)
                y = conv[:, i, :]
                link(dve.tensor_scalar(y, xc[:, 0:CV], col(2, m), None, ALU.mult))
                link(dve.scalar_tensor_tensor(y, xc[:, 1:1 + CV], col(3, m), y, ALU.mult, ALU.add))
                link(dve.scalar_tensor_tensor(y, xc[:, 2:2 + CV], col(4, m), y, ALU.mult, ALU.add))

            def times_b(j, i):
                if i:
                    dve.wait_ge(b_ready, 2 * j + i)
                done(p, j, 2, i)
                y = conv[:, i, :]
                dve.tensor_tensor(prod[:, 0:HALF], y[:, 0:HALF], psum_half(p, 2, i, 0), ALU.mult)
                dve.tensor_tensor(prod[:, HALF:NP], y[:, HALF:NP], psum_half(p, 2, i, 1, 0, H1P), ALU.mult)
                dve.tensor_tensor(prod[:, NP:N], y[:, NP + 2:CV], psum_half(p, 2, i, 1, H1P),
                                  ALU.mult).then_inc(dve_out[i], 2)
                dve.wait_ge(dve_out[i], p.out_before("d", j, 3, i))
                split_block(prod[:], B0 + 2 * j + i, b_ready)

            def gate_u(j, i):
                g = 2 * j + i
                if i:
                    dve.wait_ge(a_ready, g)
                else:
                    dve.wait_ge(b_ready, g + 2)
                dve.wait_ge(gated, g + 1)
                bias = bs_all[:, g, :]
                dve.tensor_tensor(prod[:, 0:NP].rearrange("p (c n) -> p c n", c=CH),
                                  ps_g[:, 0, :].rearrange("p (c n) -> p c n", c=CH),
                                  bias.rearrange("p (a n) -> p a n", a=1).to_broadcast((P, CH, P)), ALU.add)
                dve.tensor_tensor(prod[:, NP:N], ps_g[:, 1, 0:NS], bias[:, 0:NS], ALU.add).then_inc(gate_out, 1)
                dve.wait_ge(gate_out, g + 1)
                dve.wait_ge(act_out[i], p.out_before("a", j + 1, 0, i))
                link(dve.tensor_tensor(prod[:], prod[:], u_sb[:, i, :], ALU.mult))
                split_block(prod[:], A0 + g, a_ready)

            dve.wait_ge(bs_loaded, 16)
            dve.wait_ge(cols_ready, 1)
            before = steps[0]
            per_pass = 12
            with dve.Fori(0, 4) as j:
                loop(j, 0, before, per_pass)
                split_lo(p, j, 1)
                convolve(j, 0)
                convolve(j, 1)
                split_lo(p, j, 2)
                times_b(j, 0)
                times_b(j, 1)
                split_lo(p, j, 3)
                gate_u(j, 0)
                gate_u(j, 1)
                split_lo(p, j + 1, 0)
            steps[0] = before + 4 * per_pass

            p = ph["merge_a"]
            dve.wait_ge(staged, KD)
            dve.wait_ge(v_stored, 16)
            with dve.Fori(0, 4) as j:
                split_lo(p, j, 1)
                for i in range(2):
                    done(p, j, 1, i)
                    dve.wait_ge(act_out[i], p.out_before("a", j, 1, i))
                    dve.tensor_tensor(halves(m_a[:, 2 * j + i, :]), halves(sig[:, i, :]),
                                      ps_main[:, i, :, 0:HALF], ALU.mult).then_inc(dve_out[i], 2)
                split_lo(p, j + 1, 0)
            p = ph["merge_b"]
            before = steps[0]
            per_pass = 8
            with dve.Fori(0, 4) as j:
                loop(j, 0, before, per_pass)
                split_lo(p, j, 1)
                for i in range(2):
                    dve.wait_ge(act_out[i], p.out_before("a", j, 1, i))
                    for h in range(2):
                        cols = slice(h * HALF, (h + 1) * HALF)
                        x, block = sig[:, i, cols], M0 + 2 * j + i
                        done(p, j, 1, i, h)
                        dve.tensor_tensor(x, x, psum_half(p, 1, i, h), ALU.mult).then_inc(dve_out[i], 1)
                        dve.wait_ge(dve_out[i], p.out_before("d", j, 1, i) + h + 1)
                        link(dve.tensor_tensor(x, x, m_a[:, 2 * j + i, cols], ALU.add))
                        link(dve.tensor_copy(act_hi[:, block, cols], x))
                        dve.tensor_tensor(act_lo[:, block, cols], x, fbits(act_hi[:, block, cols]),
                                          ALU.subtract).then_inc(m_ready, 1)
                split_lo(p, j + 1, 0)
            steps[0] = before + 4 * per_pass

            p = ph["out"]
            dve.wait_ge(resid_ready, CH + 1)
            before = steps[0]
            per_pass = 8
            with dve.Fori(0, 2) as j:
                loop(j, 0, before, per_pass)
                for s in range(2):
                    if s:
                        split_lo(p, j, s)
                    for i in range(2):
                        m = 4 * j + 2 * s + i
                        for h in range(2):
                            cols = slice(h * HALF, (h + 1) * HALF)
                            x, hi, lo = (t[:, m, cols] for t in (resid, act_hi, act_lo))
                            done(p, j, s, i, h)
                            dve.tensor_tensor(x, x, psum_half(p, s, i, h), ALU.add).then_inc(dve_out[i], 1)
                            dve.wait_ge(dve_out[i], p.out_before("d", j, s, i) + h + 1)
                            link(dve.tensor_scalar(hi, x, col(5, m), None, ALU.mult))
                            dve.scalar_tensor_tensor(lo, x, col(5, m), fbits(hi), ALU.mult,
                                                     ALU.subtract).then_inc(xg_ready, 1)
                split_lo(p, j + 1, 0)
            steps[0] = before + 2 * per_pass

            dve.wait_ge(sums_turned, 1)
            dve.tensor_scalar(msq[:, 0:CH], ps_t[:, 0, 0:CH], 1.0 / D, EPS, ALU.mult, ALU.add)
            dve.tensor_scalar(msq[0:NS, CH:CH + 1], ps_t[0:NS, 0, CH:CH + 1], 1.0 / D, EPS,
                              ALU.mult, ALU.add).then_inc(msq_done, 1)
            inverse_root(CH + 3)
            for c in range(CH + 1):
                n = ROWS[c]
                dve.tensor_scalar(r_diag[0:n, c, 0:n], ident[0:n, 0:n], rstd[0:n, c:c + 1], None,
                                  ALU.mult).then_inc(diag_ready, 1)
            dve.wait_ge(r_turned, 1)
            dve.tensor_copy(r_all[:, 0:NP], ps_g[:, 0, :])
            dve.tensor_copy(r_all[:, NP:N], ps_g[:, 1, 0:NS]).then_inc(r_ready, 1)
            dve.wait_ge(r_ready, 1)

            def hidden(p, j, f0):
                for i in range(2):
                    done(p, j, 0, i)
                    dve.tensor_tensor(halves(gate_sb[:, i, :]), ps_main[:, i, :, 0:HALF],
                                      halves(r_all[:]), ALU.mult).then_inc(dve_out[i], 2)
                split_lo(p, j, 1)
                for i in range(2):
                    block = H0 + 2 * j + i
                    for h in range(2):
                        cols = slice(h * HALF, (h + 1) * HALF)
                        x = up_sb[:, cols]
                        done(p, j, 1, i, h)
                        dve.tensor_tensor(x, psum_half(p, 1, i, h), r_all[:, cols], ALU.mult).then_inc(dve_out[i], 1)
                        dve.wait_ge(dve_out[i], p.out_before("d", j, 1, i) + h + 1)
                        if h == 0:
                            dve.wait_ge(silu_done, f0 + 2 * j + i + 1)
                        link(dve.tensor_tensor(x, x, gate_sb[:, i, cols], ALU.mult))
                        link(dve.tensor_copy(act_hi[:, block, cols], x))
                        dve.tensor_tensor(act_lo[:, block, cols], x, fbits(act_hi[:, block, cols]),
                                          ALU.subtract).then_inc(h_ready, 1)
                split_lo(p, j + 1, 0)

            p = ph["ffn_1"]
            before = steps[0]
            per_pass = 8
            with dve.Fori(0, NF1 // 2) as j:
                loop(j, 0, before, per_pass)
                hidden(p, j, 0)
            steps[0] = before + NF1 // 2 * per_pass

            p = ph["down_1"]
            with dve.Fori(0, 4) as j:
                for s in range(2):
                    if s:
                        split_lo(p, j, s)
                    x = halves(resid[:, 2 * j + s, :])
                    done(p, j, s, 0)
                    dve.tensor_tensor(x, x, ps_main[:, s, :, 0:HALF], ALU.add).then_inc(dve_out[s], 2)
                split_lo(p, j + 1, 0)

            p = ph["ffn_2"]
            before = steps[0]
            with dve.Fori(0, NF2 // 2) as j:
                loop(j, 0, before, per_pass)
                hidden(p, j, NF1)
            steps[0] = before + NF2 // 2 * per_pass

            p = ph["down_2"]

            def take_x2(j, s):
                for h in range(2):
                    cols = slice(h * HALF, (h + 1) * HALF)
                    done(p, j, s, 0, h)
                    dve.tensor_tensor(x_last[:, s, cols], resid[:, 2 * j + s, cols], psum_half(p, s, 0, h),
                                      ALU.add).then_inc(dve_out[s], 1)

            def take_y(j, s):
                m = 2 * j + s
                dve.wait_ge(y_turned, m + 1)
                dve.tensor_copy(tok[:, 0:CH, bass.ds(P * m, P)], ps_misc[s][:, 0, :].rearrange("p (c n) -> p c n", c=CH))
                dve.tensor_copy(tok[0:NS, CH, bass.ds(P * m, P)], ps_misc[s][0:NS, 1, 0:P]).then_inc(y_in_tok, 1)

            take_x2(0, 0)
            with dve.Fori(0, 3) as j:
                split_lo(p, j, 1)
                take_x2(j, 1)
                take_y(j, 0)
                split_lo(p, j + 1, 0)
                take_x2(j + 1, 0)
                take_y(j, 1)
            take_x2(3, 1)
            take_y(3, 0)
            take_y(3, 1)
            dve.wait_ge(ysq_done, KD)
            dve.tensor_reduce(sumsq[:], sumsq_m[:], mybir.AxisListType.X, ALU.add).then_inc(ysum_done, 1)
            dve.wait_ge(ysum_done, 1)
            dve.tensor_scalar(msq[:], sumsq[:], 1.0 / D, EPS, ALU.mult, ALU.add).then_inc(msq_done, 1)
            inverse_root(CH + 4)
            dve.wait_ge(gf_loaded, 16)
            for c in range(CH + 1):
                n = ROWS[c]
                dve.scalar_tensor_tensor(tok[0:n, c, :], tok[0:n, c, :], rstd[0:n, c:c + 1], gf_all[0:n, :],
                                         ALU.mult, ALU.mult).then_inc(y_ready, 1)

        @block.gpsimd
        def _(pool):
            pool.memset(sumsq[:], 1.0).then_inc(stats_set, 1)
            pool.memset(msq[:], 1.0).then_inc(stats_set, 1)
            pool.memset(root[:], 1.0).then_inc(stats_set, 1)
            pool.memset(rstd[:], 1.0).then_inc(stats_set, 1)
            pool.memset(ident[:], 0.0).then_inc(zero_set, 1)
            pool.memset(ones[:], 1.0).then_inc(consts_ready, 1)
            pool.wait_ge(zero_set, 1)
            pool.affine_select(out=ident[:], in_=ident[:], compare_op=ALU.not_equal, fill=1.0, base=0,
                               pattern=[[-1, P]], channel_multiplier=1).then_inc(consts_ready, 1)
            pool.memset(meanvar[:], 1.0).then_inc(pads_ready, 1)
            pool.memset(sumsq_m[:], 1.0).then_inc(pads_ready, 1)
            pool.memset(xc[:, 0:2], 0.0).then_inc(pads_ready, 1)

            for n, loaded in enumerate((raw_loaded[0], first_loaded)):
                part = slice(n * UNIT // 2, (n + 1) * UNIT // 2)
                pool.wait_ge(loaded, 16)
                pool.tensor_copy(w_hi[:, 0, part], w_raw[:, 0, part]).then_inc(first_hi, 1)
                pool.wait_ge(first_hi, n + 1)
                pool.tensor_tensor(w_lo[:, 0, part], w_raw[:, 0, part], fbits(w_hi[:, 0, part]),
                                   ALU.subtract).then_inc(first_lo, 1)

            pool.wait_ge(ws_copied, 1)
            pool.affine_select(out=ws_t[:], in_=ws_t[:], compare_op=ALU.is_ge, fill=0.0, base=0,
                               pattern=[[0, KD], [1, P]], channel_multiplier=-1).then_inc(ws_ready, 1)

            pool.wait_ge(ln_loaded, 32)
            for c in range(CH + 1):
                n = ROWS[c]
                pool.wait_ge(v_centred, c + 1)
                pool.tensor_tensor(tok[0:n, c, :], tok[0:n, c, :], lng_all[0:n, :], ALU.mult).then_inc(v_step, 1)
                pool.wait_ge(v_step, c + 1)
                pool.tensor_tensor(tok[0:n, c, :], tok[0:n, c, :], lnb_all[0:n, :], ALU.add).then_inc(v_ready, 1)

            def stage(g):
                pool.tensor_copy(v_stage[:, 0:CH, :], tok[:, 0:CH, bass.ds(P * g, P)])
                pool.tensor_copy(v_stage[0:NS, CH, :], tok[0:NS, CH, bass.ds(P * g, P)])
                pool.tensor_copy(ws_stage[:], ws_t[:, g, :]).then_inc(staged, 1)

            pool.wait_ge(v_ready, CH + 1)
            pool.wait_ge(ws_ready, 1)
            stage(0)
            with pool.Fori(1, KD) as g:
                pool.wait_ge(gated, g)
                pool.wait_ge(staged, g)
                stage(g)

            pool.wait_ge(gate_out, KD)
            pool.dma_start(x_again[:], x_prompt[0, 0:P, :]).then_inc(again_loaded, 16)
            with pool.Fori(1, CH) as c:
                pool.wait_ge(x_turned, c)
                pool.dma_start(x_again[:], x_prompt[0, bass.ds(P * c, P), :]).then_inc(again_loaded, 16)
            pool.wait_ge(x_turned, CH)
            pool.dma_start(x_again[0:NS, :], x_sample[0]).then_inc(again_loaded, 16)

            p = ph["out"]
            pool.wait_ge(m_ready, 2 * KD)
            pool.memset(sq_sum[:], 0.0).then_inc(sum_done, 1)

            def add_square(j, s, i):
                m = 4 * j + 2 * s + i
                pool.wait_ge(dve_out[i], p.out_before("d", j, s, i) + 2)
                pool.wait_ge(sum_done, m + 1)
                pool.tensor_tensor(sq_one[:], resid[:, m, :], resid[:, m, :], ALU.mult).then_inc(sq_done, 1)
                pool.wait_ge(sq_done, m + 1)
                pool.tensor_tensor(sq_sum[:], sq_sum[:], sq_one[:], ALU.add).then_inc(sum_done, 1)

            with pool.Fori(0, 2) as j:
                for s in range(2):
                    for i in range(2):
                        add_square(j, s, i)


INS = ["x_prompt", "x_sample", "state_conv", "norm_mix", "w_in", "gmlp_ln_g", "gmlp_ln_b", "w_s", "b_s",
       "conv_w", "w_pa", "w_pb", "w_o", "norm_ffn", "w_gate", "w_up", "w_down", "norm_final"]


def kernel(**inputs):
    import numpy as _np
    import concourse.bacc as _bacc
    from concourse import mybir as _mybir
    from concourse.bass_utils import run_bass_kernel_spmd as _run

    nc = _bacc.Bacc("TRN2", target_bir_lowering=False, num_devices=1)
    arrays, args = {}, []
    for name in INS:
        a = _np.ascontiguousarray(inputs[name])
        arrays[f"in_{name}_dram"] = a
        args.append(nc.dram_tensor(f"in_{name}_dram", a.shape, _mybir.dt.from_np(a.dtype), kind="ExternalInput").ap())
    xp, xs, st = (inputs[n].shape for n in ("x_prompt", "x_sample", "state_conv"))
    outs = [xp, xs, (st[0], xp[0]) + tuple(st[2:]), st, (st[0],) + tuple(xs)]
    for i, shape in enumerate(outs):
        args.append(nc.dram_tensor(f"out_{i}_dram", tuple(shape), _mybir.dt.float32, kind="ExternalOutput").ap())
    trunk_kernel(nc, *args)
    r = _run(nc, [arrays], core_ids=[0])
    return tuple(r.results[0][f"out_{i}_dram"] for i in range(len(outs)))
```

```python
from contextlib import ExitStack

import concourse.bass as bass
from concourse import mybir

F32 = mybir.dt.float32
F32R = mybir.dt.float32r
ALU = mybir.AluOpType
ACT = mybir.ActivationFunctionType

P = 128
EPS = 1e-6

PHASES = {
    "v": (1, 4, 2),
    "mix": (4, 4, 2),
    "merge_a": (4, 2, 2),
    "merge_b": (4, 2, 2),
    "out": (2, 2, 2),
    "ffn_1": (6, 2, 2),
    "down_1": (4, 2, 1),
    "ffn_2": (5, 2, 2),
    "down_2": (4, 2, 1),
}


class Phase:

    def __init__(self, name, unit0, tile0, taken):
        self.name = name
        self.iters, self.units, self.per_unit = PHASES[name]
        self.unit0, self.tile0 = unit0, tile0
        self.taken = taken

    def in_iter(self, pair, units):
        return sum(2 for s in range(units) if self.per_unit == 2 or s % 2 == pair)

    def unit(self, j, s):
        return self.unit0 + s + self.units * j

    def loads(self, j, s):
        return (self.unit0 + s) // 2 + 1 + self.units // 2 * j

    def tile(self, j, s, i=0):
        return self.tile0 + s * self.per_unit + i + self.units * self.per_unit * j

    def pair(self, s, i):
        return i if self.per_unit == 2 else s % 2

    def out_before(self, j, s, i=0):
        p = self.pair(s, i)
        return self.taken[p] + self.in_iter(p, s) + self.in_iter(p, self.units) * j


def make_phases():
    unit, tile, taken, made = 0, 0, [0, 0], {}
    for name in PHASES:
        ph = made[name] = Phase(name, unit, tile, tuple(taken))
        unit += ph.iters * ph.units
        tile += ph.iters * ph.units * ph.per_unit
        for p in range(2):
            taken[p] += ph.in_iter(p, ph.units) * ph.iters
    return made


def trunk_kernel(nc, x_prompt, x_sample, state_conv, norm_mix, w_in, ln_g, ln_b, w_s, b_s, conv_w,
                 w_pa, w_pb, w_o, norm_ffn, w_gate, w_up, w_down, norm_final,
                 y_prompt, y_sample, conv_prompt, conv_sample, v_sample):
    D = w_in.shape[1]
    NP, NS = x_prompt.shape[1], x_sample.shape[1]
    N = NP + NS
    HALF = N // 2
    KD = D // P
    NF = w_gate.shape[2] // P
    NF1 = 2 * PHASES["ffn_1"][0]
    NF2 = NF - NF1
    CH = NP // P
    ROWS = [P] * CH + [NS]
    UNIT = KD * 2 * P
    XC = N + 4
    CV = XC - 2
    POOL_V = 4
    ACT_Y = (1, 3)
    H1P = NP - HALF
    ph = make_phases()

    ctx = ExitStack()
    with ctx:
        start = (nc.sbuf_base + 63) // 64 * 64
        place = [start]

        def sb(name, shape, dt=F32, at=None):
            size = 4
            for n in shape[1:]:
                size *= n
            off = place[0] if at is None else at
            t = nc.alloc_sbuf_tensor_at(name, shape, dt, offset=off)
            if at is None:
                place[0] = off + (size + 31) // 32 * 32
            return t, off

        w_raw, _ = sb("w_raw", [P, 2, UNIT])
        w_hi, _ = sb("w_hi", [P, 2, UNIT], F32R)
        w_lo, _ = sb("w_lo", [P, 2, UNIT], F32R)
        act_hi, hi_at = sb("act_hi", [P, 3 * KD, N], F32R)
        act_lo, lo_at = sb("act_lo", [P, 3 * KD, N], F32R)
        XN, A0, B0, M0, H0 = 0, KD, 2 * KD, KD, KD
        resid, resid_at = sb("resid", [P, KD, N])
        tok, tok_at = sb("tok", [P, CH + 1, D])
        spatial_mem, spatial_mem_at = sb("spatial_mem", [P, 2, D])
        mixer_mem, mixer_mem_at = sb("mixer_mem", [P, XC + 4 + (CH + 1) * P + P])
        ident, _ = sb("ident", [P, P])
        ones, _ = sb("ones", [P, P])
        rows48, _ = sb("rows48", [6 * KD, P])
        cols48, _ = sb("cols48", [P, 6 * KD])
        g1_cols, _ = sb("g1_cols", [P, KD])
        r_x, _ = sb("r_x", [P, N])
        r_x2, _ = sb("r_x2", [P, N])
        states, _ = sb("states", [P, 4, KD])
        states_out, _ = sb("states_out", [4 * KD, P])
        stats, _ = sb("stats", [P, CH + 1, 2, 6])
        meanvar, _ = sb("meanvar", [P, CH + 1, 2])
        sumsq, _ = sb("sumsq", [P, CH + 1])
        msq, _ = sb("msq", [P, CH + 1])
        root, _ = sb("root", [P, CH + 1])
        rstd, _ = sb("rstd", [P, CH + 1])
        newton, _ = sb("newton", [P, CH + 1])
        assert place[0] <= nc.sbuf_usable_end

        g1_rows, _ = sb("g1_rows", [KD, P], at=hi_at + A0 * N * 4)
        lng_all, _ = sb("lng_all", [P, D], at=hi_at + A0 * N * 4 + 4 * D)
        lnb_all, _ = sb("lnb_all", [P, D], at=hi_at + A0 * N * 4 + 8 * D)
        ws_in, _ = sb("ws_in", [P, KD, P], at=hi_at + A0 * N * 4 + 12 * D)
        r_diag_x, _ = sb("r_diag_x", [P, CH + 1, P], at=lo_at + A0 * N * 4)
        junk, _ = sb("junk", [P, D], at=lo_at + A0 * N * 4 + 8 * D)
        gelu_v, _ = sb("gelu_v", [P, 2, N], at=lo_at + A0 * N * 4 + 12 * D)
        gf_all, _ = sb("gf_all", [P, D], at=hi_at + (A0 + NF1) * N * 4)
        c_sb, _ = sb("c_sb", [P, 2, N], at=resid_at)
        u_sb, _ = sb("u_sb", [P, 2, N], at=resid_at + 8 * N)
        prod, _ = sb("prod", [P, N], at=resid_at + 16 * N)
        conv, _ = sb("conv", [P, 2, CV], at=resid_at + 20 * N)
        assert 20 * N + 8 * CV <= KD * N * 4
        m_a, _ = sb("m_a", [P, KD, N], at=tok_at)
        sq_sum, _ = sb("sq_sum", [P, N], at=tok_at)
        sq_one, _ = sb("sq_one", [P, N], at=tok_at + 4 * N)
        r_all, _ = sb("r_all", [P, N], at=tok_at + 8 * N)
        gate_sb, _ = sb("gate_sb", [P, 2, N], at=tok_at + 12 * N)
        up_sb, _ = sb("up_sb", [P, N], at=tok_at + 20 * N)
        r_diag, _ = sb("r_diag", [P, CH + 1, P], at=tok_at + 24 * N)
        ws_t, _ = sb("ws_t", [P, KD, P], at=spatial_mem_at)
        bs_all, _ = sb("bs_all", [P, KD, P], at=spatial_mem_at + 4 * D)
        y_sq, _ = sb("y_sq", [P, 2, N], at=spatial_mem_at)
        y_sum, _ = sb("y_sum", [P, N], at=spatial_mem_at + 8 * N)
        assert 12 * N <= 8 * D
        xc, _ = sb("xc", [P, XC], at=mixer_mem_at)
        v_stage, _ = sb("v_stage", [P, CH + 1, P], at=mixer_mem_at + 4 * (XC + 4))
        ws_stage, _ = sb("ws_stage", [P, P], at=mixer_mem_at + 4 * (XC + 4 + (CH + 1) * P))
        sig, _ = sb("sig", [P, 2, N], at=mixer_mem_at)
        x_last, _ = sb("x_last", [P, 2, N], at=mixer_mem_at)

        ps_main = ctx.enter_context(nc.psum_tensor("ps_main", [P, 2, 2, 512], F32))
        ps_t = ctx.enter_context(nc.psum_tensor("ps_t", [P, 2, 512], F32))
        ps_g = ctx.enter_context(nc.psum_tensor("ps_g", [P, 2, 512], F32))
        ps_misc = [ps_t, ps_g]
        ps_blocks = [t[:].rearrange("p b (m n) -> p (b m) n", n=P) for t in ps_misc]
        first_pair = ps_main[:, 0, :, :].rearrange("p b (m n) -> p (b m) n", n=P)
        x_blocks = [ps_blocks[0], ps_blocks[1], first_pair, ps_blocks[0], ps_blocks[1]]

        def sem(name):
            return ctx.enter_context(nc.semaphore(name))

        raw_loaded = [sem(f"raw_loaded{n}") for n in range(2)]
        first_loaded = sem("first_loaded")
        x_loaded = [sem(f"x_loaded{c}") for c in range(CH + 1)]
        g1_loaded = sem("g1_loaded")
        rows_loaded = sem("rows_loaded")
        ws_loaded = sem("ws_loaded")
        bs_loaded = sem("bs_loaded")
        ln_loaded = sem("ln_loaded")
        gf_loaded = sem("gf_loaded")
        stored = sem("stored")
        v_stored = sem("v_stored")

        hi_ready = sem("hi_ready")
        lo_ready = sem("lo_ready")
        first_hi = sem("first_hi")
        first_lo = sem("first_lo")
        tile_half = sem("tile_half")
        dve_out = [sem(f"dve_out{p}") for p in range(2)]

        g1_turned = sem("g1_turned")
        g1_ready = sem("g1_ready")
        zero_set = sem("zero_set")
        stats_set = sem("stats_set")
        consts_ready = sem("consts_ready")
        pads_ready = sem("pads_ready")
        rows_turned = sem("rows_turned")
        cols_ready = sem("cols_ready")
        ws_turned = sem("ws_turned")
        ws_copied = sem("ws_copied")
        ws_ready = sem("ws_ready")
        squares_done = sem("squares_done")
        msq_done = sem("msq_done")
        root_done = sem("root_done")
        x_turned = sem("x_turned")
        x_diag = sem("x_diag")
        rx_spread = sem("rx_spread")
        rx_ready = sem("rx_ready")
        gelu_done = sem("gelu_done")
        u_done = sem("u_done")
        sig_done = sem("sig_done")
        x_hi = sem("x_hi")
        x_ready = sem("x_ready")
        v_turned = sem("v_turned")
        v_in_tok = sem("v_in_tok")
        stats_done = sem("stats_done")
        v_centred = sem("v_centred")
        v_step = sem("v_step")
        v_ready = sem("v_ready")
        v_ready_dve = sem("v_ready_dve")
        staged = sem("staged")
        gated = sem("gated")
        gate_out = sem("gate_out")
        b_ready = sem("b_ready")
        a_ready = sem("a_ready")
        states_copied = sem("states_copied")
        states_turned = sem("states_turned")
        states_ready = sem("states_ready")
        resid_ready = sem("resid_ready")
        m_ready = sem("m_ready")
        xg_ready = sem("xg_ready")
        sq_done = sem("sq_done")
        sum_done = sem("sum_done")
        sums_turned = sem("sums_turned")
        diag_ready = sem("diag_ready")
        r_turned = sem("r_turned")
        r_ready = sem("r_ready")
        silu_done = sem("silu_done")
        h_ready = sem("h_ready")
        rstd_ready = sem("rstd_ready")
        y_turned = sem("y_turned")
        y_in_tok = sem("y_in_tok")
        ysq_done = sem("ysq_done")
        ysum_done = sem("ysum_done")
        ysums_turned = sem("ysums_turned")
        y_ready = sem("y_ready")
        y_ready_act = sem("y_ready_act")
        dve_step = sem("dve_step")

        def halves(ap):
            return ap.rearrange("p (h n) -> p h n", h=2)

        def wait(eng, s, n):
            if not isinstance(n, int) or n > 0:
                eng.wait_ge(s, n)

        def fbits(ap):
            return ap.bitcast(F32)

        block = ctx.enter_context(nc.Block())

        @block.sync
        def _(sp):
            def row_blocks(w, rows, n, width):
                return w[0, rows, bass.ds(width * n, width)].rearrange("(k p) n -> p k n", p=P)

            def slot_free(p, j, s):
                sp.wait_ge(raw_loaded[s % 2], 16)
                sp.wait_ge(lo_ready, p.unit(j, s) - 2)

            def load(p, j, s, w, n):
                slot_free(p, j, s)
                dst = w_raw[:, s % 2, :].rearrange("p (k n) -> p k n", k=KD)
                sp.dma_start(dst, row_blocks(w, slice(0, D), n, 2 * P)).then_inc(raw_loaded[s % 2], 16)

            def load_down(p, j, s, row, blocks):
                slot_free(p, j, s)
                dst = w_raw[:, s % 2, 0:blocks * P].rearrange("p (k n) -> p k n", k=blocks)
                src = row_blocks(w_down, slice(row, row + blocks * P), 2 * j + s, P)
                sp.dma_start(dst, src).then_inc(raw_loaded[s % 2], 16)

            def x_rows(c):
                return x_prompt[0, c * P:(c + 1) * P, :] if c < CH else x_sample[0]

            def load_x(c):
                sp.dma_start(tok[0:ROWS[c], c, :], x_rows(c)).then_inc(x_loaded[c], 16)

            V0, BG, CG, HH, GA, GB = (n * D // (2 * P) for n in range(1, 7))
            sp.dma_start(g1_rows[:], norm_mix[0].rearrange("(m c) -> m c", c=P)).then_inc(g1_loaded, 16)
            load_x(0)
            load_x(1)
            load_x(2)
            for n, done in ((0, raw_loaded[0]), (1, first_loaded)):
                dst = w_raw[:, 0, n * UNIT // 2:(n + 1) * UNIT // 2].rearrange("p (k n) -> p k n", k=KD // 2)
                sp.dma_start(dst, row_blocks(w_in, slice(n * D // 2, (n + 1) * D // 2), V0, 2 * P)).then_inc(done, 16)
            load_x(3)
            load_x(4)
            pv = ph["v"]
            dst = w_raw[:, 1, :].rearrange("p (k n) -> p k n", k=KD)
            sp.dma_start(dst, row_blocks(w_in, slice(0, D), V0 + 1, 2 * P)).then_inc(raw_loaded[1], 16)
            r = 0
            for src, n in ((state_conv[0, 0].rearrange("w (m c) -> (w m) c", c=P), 2 * KD),
                           (conv_w[0].rearrange("w (m c) -> (w m) c", c=P), 3 * KD),
                           (norm_ffn[0].rearrange("(m c) -> m c", c=P), KD)):
                sp.dma_start(rows48[r:r + n, :], src).then_inc(rows_loaded, 16)
                r += n
            sp.dma_start(ws_in[:], w_s[0].rearrange("g i j -> i g j")).then_inc(ws_loaded, 16)
            sp.dma_start(bs_all[:].rearrange("p g i -> p (g i)"),
                         b_s.rearrange("a g i -> a (g i)").to_broadcast((P, D))).then_inc(bs_loaded, 16)
            sp.dma_start(lng_all[:], ln_g[0:1, :].to_broadcast((P, D))).then_inc(ln_loaded, 16)
            sp.dma_start(lnb_all[:], ln_b[0:1, :].to_broadcast((P, D))).then_inc(ln_loaded, 16)
            sp.wait_ge(first_lo, 2)
            sp.dma_start(w_raw[:, 0, :].rearrange("p (k n) -> p k n", k=KD),
                         row_blocks(w_in, slice(0, D), V0 + 2, 2 * P)).then_inc(raw_loaded[0], 16)
            load(pv, 0, 3, w_in, V0 + 3)
            with sp.Fori(0, 4) as j:
                for s, part in enumerate((CG, HH, BG, 0)):
                    load(ph["mix"], j, s, w_in, j + part)
            sp.wait_ge(v_ready_dve, CH + 1 - POOL_V)
            sp.dma_start(v_sample[0, 0], tok[0:NS, CH, :]).then_inc(v_stored, 16)
            with sp.Fori(0, 4) as j:
                load(ph["merge_a"], j, 0, w_in, j + GA)
                load(ph["merge_a"], j, 1, w_pa, j)
            sp.wait_ge(states_ready, 1)
            sp.dma_start(conv_prompt[0, 0].rearrange("w (m c) -> (w m) c", c=P),
                         states_out[0:2 * KD, :]).then_inc(stored, 16)
            sp.dma_start(conv_sample[0, 0].rearrange("w (m c) -> (w m) c", c=P),
                         states_out[2 * KD:4 * KD, :]).then_inc(stored, 16)
            with sp.Fori(0, 4) as j:
                load(ph["merge_b"], j, 0, w_in, j + GB)
                load(ph["merge_b"], j, 1, w_pb, j)
            with sp.Fori(0, 2) as j:
                for s in range(2):
                    load(ph["out"], j, s, w_o, 2 * j + s)
            with sp.Fori(0, NF1 // 2) as j:
                load(ph["ffn_1"], j, 0, w_gate, j)
                load(ph["ffn_1"], j, 1, w_up, j)
            with sp.Fori(0, 4) as j:
                for s in range(2):
                    load_down(ph["down_1"], j, s, 0, NF1)
            gf_row = norm_final.rearrange("(a d) -> a d", a=1)
            sp.dma_start(gf_all[:], gf_row.to_broadcast((P, D))).then_inc(gf_loaded, 16)
            with sp.Fori(0, NF2 // 2) as j:
                load(ph["ffn_2"], j, 0, w_gate, j + NF1 // 2)
                load(ph["ffn_2"], j, 1, w_up, j + NF1 // 2)
            with sp.Fori(0, 4) as j:
                for s in range(2):
                    load_down(ph["down_2"], j, s, NF1 * P, NF2)
            for c in range(CH + 1):
                if c in ACT_Y:
                    sp.wait_ge(y_ready_act, ACT_Y.index(c) + 1)
                else:
                    sp.wait_ge(y_ready, c + 1 - sum(a < c for a in ACT_Y))
                dst = y_prompt[0, c * P:(c + 1) * P, :] if c < CH else y_sample[0]
                sp.dma_start(dst, tok[0:ROWS[c], c, :]).then_inc(stored, 16)
            sp.wait_ge(v_stored, 16)
            sp.wait_ge(stored, 16 * (2 + CH + 1))

        @block.tensor
        def _(pe):
            def product_half(p, j, s, i, h, blocks, x0, width, ready=None):
                pair = p.pair(s, i)
                out = ps_main[:, pair, h, 0:HALF]
                tok_h = slice(h * HALF, (h + 1) * HALF)
                for k in range(blocks):
                    if ready is not None:
                        ready(k, h)
                    at = k * width + (i * P if p.per_unit == 2 else 0)
                    whi = w_hi[:, s % 2, at:at + P]
                    wlo = w_lo[:, s % 2, at:at + P]
                    xhi, xlo = act_hi[:, x0 + k, tok_h], act_lo[:, x0 + k, tok_h]
                    pe.matmul(out, whi, xhi, start=(k == 0), stop=False)
                    pe.matmul(out, whi, xlo, start=False, stop=False)
                    last = pe.matmul(out, wlo, xhi, start=False, stop=(k == blocks - 1))
                last.then_inc(tile_half, 1)

            def pair_free(p, j, s, i):
                pair = p.pair(s, i)
                if p.name != "v" or s:
                    pe.wait_ge(dve_out[pair], p.out_before(j, s, i))

            def unit(p, j, s, x0, blocks=KD, ready=None, behind={}):
                pe.wait_ge(lo_ready, p.unit(j, s))
                for i in range(p.per_unit):
                    pair_free(p, j, s, i)
                    for h in range(2):
                        product_half(p, j, s, i, h, blocks, x0, 2 * P if p.per_unit == 2 else P,
                                     ready if i == 0 and s == 0 else None)
                        if (i, h) in behind:
                            behind[i, h]()

            def turn_blocks(out, src, rows):
                for m in range(KD):
                    last = pe.transpose(out[:, m, 0:rows], src[0:rows, m * P:(m + 1) * P], ident[0:rows, 0:rows])
                return last

            def turn_tokens(out, src):
                for c in range(CH + 1):
                    dst = out[0:P, 0, c * P:(c + 1) * P] if c < CH else out[0:NS, 1, 0:P]
                    last = pe.transpose(dst, src[:, c * P:c * P + ROWS[c]], ident[:, :])
                return last

            def spread(diag, ready, chunks, done):
                pe.wait_ge(ready, chunks)
                for c in range(CH + 1):
                    n = ROWS[c]
                    dst = ps_g[:, 0, c * P:(c + 1) * P] if c < CH else ps_g[:, 1, 0:NS]
                    last = pe.matmul(dst, ones[0:n, :], diag[0:n, c, 0:n], start=True, stop=True)
                last.then_inc(done, 1)

            pe.wait_ge(consts_ready, 2)
            pe.wait_ge(g1_loaded, 16)
            pe.transpose(ps_main[:, 1, 0, 0:KD], g1_rows[:, :], ident[0:KD, 0:KD]).then_inc(g1_turned, 1)
            for c in range(CH + 1):
                pe.wait_ge(x_loaded[c], 16)
                if c >= 3:
                    pe.wait_ge(x_ready, c - 2)
                turn_blocks(x_blocks[c], tok[:, c, :], ROWS[c]).then_inc(x_turned, 1)

            pv = ph["v"]
            pe.wait_ge(x_ready, 3)

            def first_rows(k, h):
                if k % (KD // 2) == 0:
                    pe.wait_ge(first_lo, k // (KD // 2) + 1)
            product_half(pv, 0, 0, 0, 0, KD, XN, 2 * P, first_rows)
            pe.wait_ge(x_ready, CH + 1)
            product_half(pv, 0, 0, 0, 1, KD, XN, 2 * P)
            product_half(pv, 0, 0, 1, 0, KD, XN, 2 * P)
            spread(r_diag_x, x_diag, CH + 1, rx_spread)
            product_half(pv, 0, 0, 1, 1, KD, XN, 2 * P)

            def turn_v(t):
                pe.wait_ge(gelu_done, t + 1)
                if t == 1:
                    pe.wait_ge(cols_ready, 1)
                if t == 2:
                    pe.wait_ge(ws_copied, 1)
                if t > 2:
                    pe.wait_ge(v_in_tok, t - 1)
                turn_tokens(ps_misc[t % 2], gelu_v[:, t % 2, :]).then_inc(v_turned, 1)

            for t in range(1, 2 * pv.units):
                s, i = divmod(t, 2)
                if i == 0:
                    pe.wait_ge(lo_ready, s)
                if t > 1:
                    pair_free(pv, 0, s, i)
                    for h in range(2):
                        product_half(pv, 0, s, i, h, KD, XN, 2 * P)
                turn_v(t - 1)
                if t == 1:
                    pe.wait_ge(rows_loaded, 48)
                    pe.wait_ge(rx_ready, 1)
                    pe.transpose(ps_g[:, 0, 0:6 * KD], rows48[:, :], ident[0:6 * KD, 0:6 * KD]).then_inc(rows_turned, 1)
                if t == 2:
                    pe.wait_ge(v_in_tok, 1)
                    pe.wait_ge(ws_loaded, 16)
                    for g in range(KD):
                        last = pe.transpose(ps_blocks[0][:, g, :], ws_in[:, g, :], ident[:, :])
                    last.then_inc(ws_turned, 1)

            def mix(j, behind={}):
                p = ph["mix"]

                def mix_positions(i):
                    g = 2 * j + i
                    pe.wait_ge(staged, g + 1)
                    if i == 1:
                        pe.wait_ge(gate_out, g)
                    for c in range(CH):
                        pe.matmul(ps_g[:, 0, c * P:(c + 1) * P], v_stage[:, c, :], ws_stage[:, :],
                                  start=True, stop=True)
                    pe.matmul(ps_g[:, 1, 0:NS], v_stage[0:NS, CH, :], ws_stage[0:NS, 0:NS],
                              start=True, stop=True).then_inc(gated, 1)

                unit(p, j, 0, XN, behind=behind)
                unit(p, j, 1, XN)
                unit(p, j, 2, XN)
                unit(p, j, 3, XN, behind={(0, 1): lambda: mix_positions(0), (1, 1): lambda: mix_positions(1)})

            mix(0, behind={(0, 0): lambda: turn_v(2 * pv.units - 1)})
            with pe.Fori(1, 4) as j:
                mix(j)

            pe.wait_ge(states_copied, KD)
            pe.transpose(ps_t[0:4 * KD, 0, 0:P], states[:].rearrange("p w m -> p (w m)"),
                         ident[:, :]).then_inc(states_turned, 1)

            with pe.Fori(0, 4) as j:
                p = ph["merge_a"]
                unit(p, j, 0, XN)
                pe.wait_ge(a_ready, KD)
                unit(p, j, 1, A0)
            with pe.Fori(0, 4) as j:
                p = ph["merge_b"]
                unit(p, j, 0, XN)
                pe.wait_ge(b_ready, KD)
                unit(p, j, 1, B0)
            with pe.Fori(0, 2) as j:
                p = ph["out"]
                for s in range(2):
                    unit(p, j, s, M0, ready=lambda k, h: pe.wait_ge(m_ready, 2 * k + h + 1))

            def xg_there(k, h):
                pe.wait_ge(xg_ready, 2 * k + h + 1)

            p = ph["ffn_1"]

            def norm_sums():
                pe.wait_ge(sum_done, KD + 1)
                for c in range(CH + 1):
                    last = pe.matmul(ps_t[0:ROWS[c], 0, c:c + 1], sq_sum[:, c * P:c * P + ROWS[c]],
                                     ones[:, 0:1], start=True, stop=True)
                last.then_inc(sums_turned, 1)

            unit(p, 0, 0, XN, ready=xg_there,
                 behind={(0, 1): norm_sums, (1, 0): lambda: spread(r_diag, diag_ready, CH + 1, r_turned)})
            unit(p, 0, 1, XN)
            with pe.Fori(1, NF1 // 2) as j:
                unit(p, j, 0, XN)
                unit(p, j, 1, XN)
            with pe.Fori(0, 4) as j:
                for s in range(2):
                    unit(ph["down_1"], j, s, H0, NF1, ready=lambda k, h: pe.wait_ge(h_ready, 2 * k + h + 1))
            with pe.Fori(0, NF2 // 2) as j:
                unit(ph["ffn_2"], j, 0, XN)
                unit(ph["ffn_2"], j, 1, XN)

            p = ph["down_2"]

            def down(j, s):
                unit(p, j, s, H0, NF2, ready=lambda k, h: pe.wait_ge(h_ready, 2 * NF1 + 2 * k + h + 1))

            def turn_y(j, s):
                pe.wait_ge(dve_out[s], p.out_before(j, s) + 2)
                turn_tokens(ps_misc[s], x_last[:, s, :]).then_inc(y_turned, 1)

            down(0, 0)
            with pe.Fori(0, 3) as j:
                down(j, 1)
                turn_y(j, 0)
                down(j + 1, 0)
                turn_y(j, 1)
            down(3, 1)
            turn_y(3, 0)
            turn_y(3, 1)
            pe.wait_ge(ysum_done, KD)
            pe.wait_ge(ysq_done, KD)
            for c in range(CH + 1):
                n = ROWS[c]
                out = ps_main[0:n, 0, 0, c:c + 1]
                pe.matmul(out, y_sum[:, c * P:c * P + n], ones[:, 0:1], start=True, stop=False)
                last = pe.matmul(out, y_sq[:, 1, c * P:c * P + n], ones[:, 0:1], start=False, stop=True)
            last.then_inc(ysums_turned, 1)

        @block.scalar
        def _(act):
            def split_hi(p, j, s, norm=False):
                slot = (s + 1) % 2
                act.wait_ge(raw_loaded[slot], 16 * p.loads(j, s + 1))
                wait(act, tile_half, 2 * p.tile(j, s))
                if norm:
                    hi_times_norm(slot, range(KD)).then_inc(hi_ready, 1)
                else:
                    act.copy(w_hi[:, slot, :], w_raw[:, slot, :]).then_inc(hi_ready, 1)

            def hi_times_norm(slot, blocks):
                for k in blocks:
                    at = slice(k * 2 * P, (k + 1) * 2 * P)
                    last = act.activation(w_hi[:, slot, at], w_raw[:, slot, at], ACT.Copy,
                                          scale=g1_cols[:, k:k + 1])
                return last

            act.wait_ge(stats_set, 4)
            act.activation(junk[:, 0:1], sumsq[:, 0:1], ACT.Sqrt).then_inc(squares_done, 1)
            act.wait_ge(g1_turned, 1)
            act.copy(g1_cols[:], ps_main[:, 1, 0, 0:KD]).then_inc(g1_ready, 1)
            act.wait_ge(g1_ready, 1)

            def take_x(c):
                act.wait_ge(x_turned, c + 1)
                act.copy(act_hi[:, XN:XN + KD, c * P:c * P + ROWS[c]],
                         x_blocks[c][:, :, 0:ROWS[c]]).then_inc(x_hi, 1)

            def first_unit(n, loaded):
                act.wait_ge(loaded, 16)
                hi_times_norm(0, range(n * KD // 2, (n + 1) * KD // 2)).then_inc(first_hi, 1)

            def squares(c):
                n = ROWS[c]
                act.wait_ge(x_loaded[c], 16)
                act.wait_ge(squares_done, c + 1)
                act.activation(junk[0:n, :], tok[0:n, c, :], ACT.Square,
                               accum_out=sumsq[0:n, c:c + 1]).then_inc(squares_done, 1)

            squares(0)
            take_x(0)
            take_x(1)
            first_unit(0, raw_loaded[0])
            take_x(2)
            first_unit(1, first_loaded)
            take_x(3)
            take_x(4)
            for c in range(1, CH + 1):
                squares(c)
            act.wait_ge(msq_done, 1)
            act.activation(root[:], msq[:], ACT.Sqrt).then_inc(root_done, 1)

            p = ph["v"]
            for t in range(2 * p.units):
                s, i = divmod(t, 2)
                if i == 0:
                    split_hi(p, 0, s, norm=True)
                act.wait_ge(dve_out[i], p.out_before(0, s, i) + 2)
                act.activation(gelu_v[:, i, :], gelu_v[:, i, :], ACT.Gelu).then_inc(gelu_done, 1)
                if t == 1:
                    act.wait_ge(rows_turned, 1)
                    act.copy(cols48[:], ps_g[:, 0, 0:6 * KD]).then_inc(cols_ready, 1)
                if t == 2:
                    act.wait_ge(ws_turned, 1)
                    act.copy(ws_t[:], ps_blocks[0]).then_inc(ws_copied, 1)

            p = ph["mix"]

            def mix(j):
                split_hi(p, j, 0, norm=True)
                if isinstance(j, int):
                    act.wait_ge(msq_done, 2)
                    act.activation(root[:], msq[:], ACT.Sqrt).then_inc(root_done, 1)
                split_hi(p, j, 1, norm=True)
                split_hi(p, j, 2, norm=True)
                split_hi(p, j, 3, norm=True)
                for i in range(2):
                    act.wait_ge(dve_out[i], p.out_before(j, 3, i) + 2)
                    act.activation(u_sb[:, i, :], u_sb[:, i, :], ACT.Gelu).then_inc(u_done, 1)

            mix(0)
            with act.Fori(1, 4) as j:
                mix(j)

            def sigmoids(p, j):
                split_hi(p, j, 0)
                for i in range(2):
                    act.wait_ge(dve_out[i], p.out_before(j, 0, i) + 2)
                    act.activation(sig[:, i, :], sig[:, i, :], ACT.Sigmoid).then_inc(sig_done, 1)

            p = ph["merge_a"]
            act.wait_ge(states_turned, 1)
            act.copy(states_out[:], ps_t[0:4 * KD, 0, 0:P]).then_inc(states_ready, 1)
            with act.Fori(0, 4) as j:
                sigmoids(p, j)
                split_hi(p, j, 1, norm=True)
            p = ph["merge_b"]
            with act.Fori(0, 3) as j:
                sigmoids(p, j)
                split_hi(p, j, 1, norm=True)
            sigmoids(p, 3)
            split_hi(p, 3, 1)

            with act.Fori(0, 2) as j:
                for s in range(2):
                    split_hi(ph["out"], j, s)

            def silus(p, j):
                for i in range(2):
                    act.wait_ge(dve_out[i], p.out_before(j, 0, i) + 2)
                    act.activation(gate_sb[:, i, :], gate_sb[:, i, :], ACT.Silu).then_inc(silu_done, 1)

            p = ph["ffn_1"]
            split_hi(p, 0, 0)
            act.wait_ge(msq_done, 3)
            act.activation(root[:], msq[:], ACT.Sqrt).then_inc(root_done, 1)
            silus(p, 0)
            split_hi(p, 0, 1)
            with act.Fori(1, NF1 // 2) as j:
                split_hi(p, j, 0)
                silus(p, j)
                split_hi(p, j, 1)
            with act.Fori(0, 4) as j:
                split_hi(ph["down_1"], j, 0)
                split_hi(ph["down_1"], j, 1)
            p = ph["ffn_2"]
            with act.Fori(0, NF2 // 2) as j:
                split_hi(p, j, 0)
                silus(p, j)
                split_hi(p, j, 1)

            p = ph["down_2"]

            def y_squares(j, s, first=False):
                act.wait_ge(dve_out[s], p.out_before(j, s) + 2)
                if not first:
                    act.wait_ge(ysum_done, 2 * j + s)
                act.activation(y_sq[:, s, :], x_last[:, s, :], ACT.Square).then_inc(ysq_done, 1)

            act.wait_ge(silu_done, NF)
            act.wait_ge(gate_out, KD)
            act.wait_ge(staged, KD)
            act.activation(root[:, 0:1], msq[:, 0:1], ACT.Sqrt).then_inc(root_done, 1)
            split_hi(p, 0, 0)
            split_hi(p, 0, 1)
            y_squares(0, 0, first=True)
            split_hi(p, 1, 0)
            y_squares(0, 1, first=True)
            with act.Fori(1, 3) as j:
                split_hi(p, j, 1)
                y_squares(j, 0)
                split_hi(p, j + 1, 0)
                y_squares(j, 1)
            y_squares(3, 0)
            y_squares(3, 1)
            act.wait_ge(msq_done, 4)
            act.activation(root[:], msq[:], ACT.Sqrt).then_inc(root_done, 1)
            act.wait_ge(y_in_tok, KD)
            act.wait_ge(rstd_ready, 1)
            for c in ACT_Y:
                act.activation(tok[:, c, :], tok[:, c, :], ACT.Copy, scale=rstd[:, c:c + 1]).then_inc(y_ready_act, 1)

        @block.vector
        def _(dve):
            steps = [0]

            def link(ins):
                steps[0] += 1
                ins.then_inc(dve_step, 1)
                dve.wait_ge(dve_step, steps[0])

            def loop(j, first, before, count):
                steps[0] = before + count * (j - first)

            def inverse_root(norm, last=None):
                x, r, t = msq[:], rstd[:], newton[:]
                dve.wait_ge(root_done, norm)
                link(dve.reciprocal(r, root[:]))
                link(dve.tensor_tensor(t, x, r, ALU.mult))
                link(dve.scalar_tensor_tensor(t, t, -0.5, r, ALU.mult, ALU.mult))
                end = dve.scalar_tensor_tensor(r, t, 1.5, r, ALU.add, ALU.mult)
                if last is None:
                    link(end)
                else:
                    end.then_inc(last, 1)
                    dve.wait_ge(last, 1)

            def split_lo(p, j, s, norm=False):
                slot = (s + 1) % 2
                dve.wait_ge(hi_ready, p.unit(j, s + 1))
                if norm:
                    lo_times_norm(slot, range(KD)).then_inc(lo_ready, 1)
                else:
                    dve.tensor_tensor(w_lo[:, slot, :], w_raw[:, slot, :], fbits(w_hi[:, slot, :]),
                                      ALU.subtract).then_inc(lo_ready, 1)

            def lo_times_norm(slot, blocks):
                for k in blocks:
                    at = slice(k * 2 * P, (k + 1) * 2 * P)
                    last = dve.scalar_tensor_tensor(w_lo[:, slot, at], w_raw[:, slot, at], g1_cols[:, k:k + 1],
                                                    fbits(w_hi[:, slot, at]), ALU.mult, ALU.subtract)
                return last

            def take_times_r(p, j, s, i, out, r):
                done(p, j, s, i)
                dve.tensor_tensor(halves(out), ps_main[:, i, :, 0:HALF], halves(r[:]),
                                  ALU.mult).then_inc(dve_out[i], 2)

            def psum_half(p, s, i, h, a=0, b=HALF):
                return ps_main[:, p.pair(s, i), h, a:b]

            def done(p, j, s, i, h=1):
                dve.wait_ge(tile_half, 2 * p.tile(j, s, i) + h + 1)

            def take_x(c):
                dve.wait_ge(x_hi, c + 1)
                cols = slice(c * P, c * P + ROWS[c])
                dve.tensor_tensor(act_lo[:, XN:XN + KD, cols], x_blocks[c][:, :, 0:ROWS[c]],
                                  fbits(act_hi[:, XN:XN + KD, cols]), ALU.subtract).then_inc(x_ready, 1)

            def first_unit(n):
                dve.wait_ge(first_hi, n + 1)
                lo_times_norm(0, range(n * KD // 2, (n + 1) * KD // 2)).then_inc(first_lo, 1)

            dve.wait_ge(stats_set, 4)
            take_x(0)
            take_x(1)
            first_unit(0)
            take_x(2)
            first_unit(1)
            take_x(3)
            take_x(4)

            def diagonals(diag, signal):
                for c in range(CH + 1):
                    n = ROWS[c]
                    dve.tensor_scalar(diag[0:n, c, 0:n], ident[0:n, 0:n], rstd[0:n, c:c + 1], None,
                                      ALU.mult).then_inc(signal, 1)

            dve.wait_ge(squares_done, CH + 2)
            dve.tensor_scalar(msq[:], sumsq[:], 1.0 / D, EPS, ALU.mult, ALU.add).then_inc(msq_done, 1)
            inverse_root(1)
            diagonals(r_diag_x, x_diag)
            split_lo(ph["v"], 0, 0, norm=True)
            dve.wait_ge(rx_spread, 1)
            dve.tensor_copy(r_x[:, 0:NP], ps_g[:, 0, :])
            dve.tensor_copy(r_x[:, NP:N], ps_g[:, 1, 0:NS]).then_inc(rx_ready, 1)
            dve.wait_ge(rx_ready, 1)
            dve.tensor_tensor(r_x2[:], r_x[:], r_x[:], ALU.mult).then_inc(rx_ready, 1)
            dve.wait_ge(rx_ready, 2)

            p = ph["v"]

            def take_v(t):
                dve.wait_ge(v_turned, t + 1)
                dve.tensor_copy(tok[:, 0:CH, t * P:(t + 1) * P],
                                ps_misc[t % 2][:, 0, :].rearrange("p (c n) -> p c n", c=CH))
                dve.tensor_copy(tok[0:NS, CH, t * P:(t + 1) * P], ps_misc[t % 2][0:NS, 1, 0:P]).then_inc(v_in_tok, 1)

            def v_stats(part):
                dve.wait_ge(v_in_tok, KD // 2 * (part + 1))
                for c in range(CH + 1):
                    n = ROWS[c]
                    last = dve.bn_stats(stats[0:n, c, part, :], tok[0:n, c, part * D // 2:(part + 1) * D // 2])
                last.then_inc(stats_done, 1)

            for t in range(2 * p.units):
                s, i = divmod(t, 2)
                if i == 0 and s:
                    split_lo(p, 0, s, norm=True)
                if t >= 2:
                    dve.wait_ge(v_turned, t - 1)
                take_times_r(p, 0, s, i, gelu_v[:, i, :], r_x)
                if t:
                    take_v(t - 1)
                if t == 5:
                    v_stats(0)
            take_v(KD - 1)
            mix = ph["mix"]
            split_lo(mix, 0, 0, norm=True)
            take_times_r(mix, 0, 0, 0, c_sb[:, 0, :], r_x2)
            v_stats(1)
            dve.wait_ge(stats_done, 2)
            dve.wait_ge(pads_ready, 2)
            for c in range(CH + 1):
                last = dve.bn_aggr(meanvar[0:ROWS[c], c, :], stats[0:ROWS[c], c, :, :])
            link(last)
            dve.tensor_scalar(msq[:], meanvar[:, :, 1], EPS, None, ALU.add).then_inc(msq_done, 1)
            inverse_root(2)
            for c in range(POOL_V):
                n = ROWS[c]
                dve.tensor_scalar(tok[0:n, c, :], tok[0:n, c, :], meanvar[0:n, c, 0:1], rstd[0:n, c:c + 1],
                                  ALU.subtract, ALU.mult).then_inc(v_centred, 1)
            take_times_r(mix, 0, 0, 1, c_sb[:, 1, :], r_x2)
            dve.wait_ge(ln_loaded, 32)
            for c in range(POOL_V, CH + 1):
                n = ROWS[c]
                v = tok[0:n, c, :]
                link(dve.scalar_tensor_tensor(v, v, meanvar[0:n, c, 0:1], lng_all[0:n, :], ALU.subtract, ALU.mult))
                dve.scalar_tensor_tensor(v, v, rstd[0:n, c:c + 1], lnb_all[0:n, :],
                                         ALU.mult, ALU.add).then_inc(v_ready_dve, 1)

            p = mix

            def split_block(x, block, signal):
                link(dve.tensor_copy(act_hi[:, block, :], x))
                dve.tensor_tensor(act_lo[:, block, :], x, fbits(act_hi[:, block, :]), ALU.subtract).then_inc(signal, 1)

            def col(n, m):
                return cols48[:, bass.ds(n * KD + m, 1)]

            def convolve(j, i):
                m = 2 * j + i
                dve.tensor_copy(xc[:, NP + 2:NP + 4], cols48[:, 0:2 * KD].rearrange("p (w m) -> p w m", w=2)[:, :, m])
                done(p, j, 1, i)
                dve.wait_ge(dve_out[i], p.out_before(j, 1, i))
                c = c_sb[:, i, :]
                dve.tensor_tensor(xc[:, 2:2 + HALF], c[:, 0:HALF], psum_half(p, 1, i, 0), ALU.mult)
                dve.tensor_tensor(xc[:, 2 + HALF:2 + NP], c[:, HALF:NP], psum_half(p, 1, i, 1, 0, H1P), ALU.mult)
                dve.tensor_tensor(xc[:, NP + 4:N + 4], c[:, NP:N], psum_half(p, 1, i, 1, H1P),
                                  ALU.mult).then_inc(dve_out[i], 2)
                dve.wait_ge(dve_out[i], p.out_before(j, 2, i))
                dve.tensor_copy(states[:, 0:2, m], xc[:, NP:NP + 2])
                dve.tensor_copy(states[:, 2:4, m], xc[:, N + 2:N + 4]).then_inc(states_copied, 1)
                y = conv[:, i, :]
                link(dve.tensor_scalar(y, xc[:, 0:CV], col(2, m), None, ALU.mult))
                link(dve.scalar_tensor_tensor(y, xc[:, 1:1 + CV], col(3, m), y, ALU.mult, ALU.add))
                link(dve.scalar_tensor_tensor(y, xc[:, 2:2 + CV], col(4, m), y, ALU.mult, ALU.add))

            def times_b(j, i):
                if i:
                    dve.wait_ge(b_ready, 2 * j + i)
                done(p, j, 2, i)
                y = conv[:, i, :]
                dve.tensor_tensor(prod[:, 0:HALF], y[:, 0:HALF], psum_half(p, 2, i, 0), ALU.mult)
                dve.tensor_tensor(prod[:, HALF:NP], y[:, HALF:NP], psum_half(p, 2, i, 1, 0, H1P), ALU.mult)
                dve.tensor_tensor(prod[:, NP:N], y[:, NP + 2:CV], psum_half(p, 2, i, 1, H1P),
                                  ALU.mult).then_inc(dve_out[i], 2)
                dve.wait_ge(dve_out[i], p.out_before(j, 3, i))
                link(dve.tensor_tensor(prod[:], prod[:], r_x[:], ALU.mult))
                split_block(prod[:], B0 + 2 * j + i, b_ready)

            def gate_u(j, i):
                g = 2 * j + i
                if i:
                    dve.wait_ge(a_ready, g)
                else:
                    dve.wait_ge(b_ready, g + 2)
                dve.wait_ge(gated, g + 1)
                bias = bs_all[:, g, :]
                dve.tensor_tensor(prod[:, 0:NP].rearrange("p (c n) -> p c n", c=CH),
                                  ps_g[:, 0, :].rearrange("p (c n) -> p c n", c=CH),
                                  bias.rearrange("p (a n) -> p a n", a=1).to_broadcast((P, CH, P)), ALU.add)
                dve.tensor_tensor(prod[:, NP:N], ps_g[:, 1, 0:NS], bias[:, 0:NS], ALU.add).then_inc(gate_out, 1)
                dve.wait_ge(gate_out, g + 1)
                dve.wait_ge(u_done, g + 1)
                link(dve.tensor_tensor(prod[:], prod[:], u_sb[:, i, :], ALU.mult))
                split_block(prod[:], A0 + g, a_ready)

            dve.wait_ge(bs_loaded, 16)
            dve.wait_ge(cols_ready, 1)
            before = steps[0]
            per_pass = 14

            def mixers(j, first=False, last=False):
                loop(j, 0, before, per_pass)
                if not first:
                    take_times_r(p, j, 0, 0, c_sb[:, 0, :], r_x2)
                    take_times_r(p, j, 0, 1, c_sb[:, 1, :], r_x2)
                split_lo(p, j, 1, norm=True)
                convolve(j, 0)
                convolve(j, 1)
                split_lo(p, j, 2, norm=True)
                times_b(j, 0)
                times_b(j, 1)
                split_lo(p, j, 3, norm=True)
                for i in range(2):
                    take_times_r(p, j, 3, i, u_sb[:, i, :], r_x)
                    gate_u(j, i)
                split_lo(p, j + 1, 0, norm=not last)

            mixers(0, first=True)
            with dve.Fori(1, 3) as j:
                mixers(j)
            mixers(3, last=True)
            steps[0] = before + 4 * per_pass

            p = ph["merge_a"]
            dve.wait_ge(staged, KD)
            dve.wait_ge(v_stored, 16)
            dve.wait_ge(a_ready, KD)
            with dve.Fori(0, 4) as j:
                take_times_r(p, j, 0, 0, sig[:, 0, :], r_x)
                take_times_r(p, j, 0, 1, sig[:, 1, :], r_x)
                split_lo(p, j, 1, norm=True)
                for i in range(2):
                    done(p, j, 1, i)
                    dve.wait_ge(sig_done, 2 * j + i + 1)
                    dve.tensor_tensor(halves(m_a[:, 2 * j + i, :]), halves(sig[:, i, :]),
                                      ps_main[:, i, :, 0:HALF], ALU.mult).then_inc(dve_out[i], 2)
                split_lo(p, j + 1, 0)
            p = ph["merge_b"]
            before = steps[0]
            per_pass = 8

            def merge_b(j, first=False, last=False):
                loop(j, 0, before, per_pass)
                if not first:
                    dve.wait_ge(m_ready, 4 * j)
                for i in range(2):
                    take_times_r(p, j, 0, i, sig[:, i, :], r_x)
                split_lo(p, j, 1, norm=not last)
                for i in range(2):
                    dve.wait_ge(sig_done, KD + 2 * j + i + 1)
                    for h in range(2):
                        cols = slice(h * HALF, (h + 1) * HALF)
                        x, block = sig[:, i, cols], M0 + 2 * j + i
                        done(p, j, 1, i, h)
                        dve.tensor_tensor(x, x, psum_half(p, 1, i, h), ALU.mult).then_inc(dve_out[i], 1)
                        dve.wait_ge(dve_out[i], p.out_before(j, 1, i) + h + 1)
                        link(dve.tensor_tensor(x, x, m_a[:, 2 * j + i, cols], ALU.add))
                        link(dve.tensor_copy(act_hi[:, block, cols], x))
                        dve.tensor_tensor(act_lo[:, block, cols], x, fbits(act_hi[:, block, cols]),
                                          ALU.subtract).then_inc(m_ready, 1)
                split_lo(p, j + 1, 0)

            merge_b(0, first=True)
            with dve.Fori(1, 3) as j:
                merge_b(j)
            merge_b(3, last=True)
            steps[0] = before + 4 * per_pass

            p = ph["out"]
            dve.wait_ge(resid_ready, 1)
            before = steps[0]
            per_pass = 8
            with dve.Fori(0, 2) as j:
                loop(j, 0, before, per_pass)
                for s in range(2):
                    if s:
                        split_lo(p, j, s)
                    for i in range(2):
                        m = 4 * j + 2 * s + i
                        for h in range(2):
                            cols = slice(h * HALF, (h + 1) * HALF)
                            x, hi, lo = (t[:, m, cols] for t in (resid, act_hi, act_lo))
                            done(p, j, s, i, h)
                            dve.tensor_tensor(x, x, psum_half(p, s, i, h), ALU.add).then_inc(dve_out[i], 1)
                            dve.wait_ge(dve_out[i], p.out_before(j, s, i) + h + 1)
                            link(dve.tensor_scalar(hi, x, col(5, m), None, ALU.mult))
                            dve.scalar_tensor_tensor(lo, x, col(5, m), fbits(hi), ALU.mult,
                                                     ALU.subtract).then_inc(xg_ready, 1)
                split_lo(p, j + 1, 0)
            steps[0] = before + 2 * per_pass

            dve.wait_ge(sums_turned, 1)
            dve.tensor_scalar(msq[:, 0:CH], ps_t[:, 0, 0:CH], 1.0 / D, EPS, ALU.mult, ALU.add)
            dve.tensor_scalar(msq[0:NS, CH:CH + 1], ps_t[0:NS, 0, CH:CH + 1], 1.0 / D, EPS,
                              ALU.mult, ALU.add).then_inc(msq_done, 1)
            inverse_root(3)
            diagonals(r_diag, diag_ready)
            dve.wait_ge(r_turned, 1)
            dve.tensor_copy(r_all[:, 0:NP], ps_g[:, 0, :])
            dve.tensor_copy(r_all[:, NP:N], ps_g[:, 1, 0:NS]).then_inc(r_ready, 1)
            dve.wait_ge(r_ready, 1)

            def hidden(p, j, f0):
                for i in range(2):
                    done(p, j, 0, i)
                    dve.tensor_tensor(halves(gate_sb[:, i, :]), ps_main[:, i, :, 0:HALF],
                                      halves(r_all[:]), ALU.mult).then_inc(dve_out[i], 2)
                split_lo(p, j, 1)
                for i in range(2):
                    block = H0 + 2 * j + i
                    for h in range(2):
                        cols = slice(h * HALF, (h + 1) * HALF)
                        x = up_sb[:, cols]
                        done(p, j, 1, i, h)
                        dve.tensor_tensor(x, psum_half(p, 1, i, h), r_all[:, cols], ALU.mult).then_inc(dve_out[i], 1)
                        dve.wait_ge(dve_out[i], p.out_before(j, 1, i) + h + 1)
                        if h == 0:
                            dve.wait_ge(silu_done, f0 + 2 * j + i + 1)
                        link(dve.tensor_tensor(x, x, gate_sb[:, i, cols], ALU.mult))
                        link(dve.tensor_copy(act_hi[:, block, cols], x))
                        dve.tensor_tensor(act_lo[:, block, cols], x, fbits(act_hi[:, block, cols]),
                                          ALU.subtract).then_inc(h_ready, 1)
                split_lo(p, j + 1, 0)

            p = ph["ffn_1"]
            before = steps[0]
            per_pass = 8
            with dve.Fori(0, NF1 // 2) as j:
                loop(j, 0, before, per_pass)
                hidden(p, j, 0)
            steps[0] = before + NF1 // 2 * per_pass

            p = ph["down_1"]
            with dve.Fori(0, 4) as j:
                for s in range(2):
                    if s:
                        split_lo(p, j, s)
                    x = halves(resid[:, 2 * j + s, :])
                    done(p, j, s, 0)
                    dve.tensor_tensor(x, x, ps_main[:, s, :, 0:HALF], ALU.add).then_inc(dve_out[s], 2)
                split_lo(p, j + 1, 0)

            p = ph["ffn_2"]
            before = steps[0]
            with dve.Fori(0, NF2 // 2) as j:
                loop(j, 0, before, per_pass)
                hidden(p, j, NF1)
            steps[0] = before + NF2 // 2 * per_pass

            p = ph["down_2"]

            def take_x2(j, s, first=False):
                if not first:
                    dve.wait_ge(ysq_done, 2 * j + s - 1)
                for h in range(2):
                    cols = slice(h * HALF, (h + 1) * HALF)
                    done(p, j, s, 0, h)
                    dve.tensor_tensor(x_last[:, s, cols], resid[:, 2 * j + s, cols], psum_half(p, s, 0, h),
                                      ALU.add).then_inc(dve_out[s], 1)

            def take_y(j, s):
                m = 2 * j + s
                dve.wait_ge(y_turned, m + 1)
                gf = gf_all[:, bass.ds(P * m, P)]
                dve.tensor_tensor(tok[:, 0:CH, bass.ds(P * m, P)],
                                  ps_misc[s][:, 0, :].rearrange("p (c n) -> p c n", c=CH),
                                  gf.rearrange("p (a n) -> p a n", a=1).to_broadcast((P, CH, P)), ALU.mult)
                dve.tensor_tensor(tok[0:NS, CH, bass.ds(P * m, P)], ps_misc[s][0:NS, 1, 0:P], gf[0:NS],
                                  ALU.mult).then_inc(y_in_tok, 1)

            dve.wait_ge(gf_loaded, 16)
            take_x2(0, 0, first=True)
            split_lo(p, 0, 1)
            take_x2(0, 1, first=True)
            take_y(0, 0)
            split_lo(p, 1, 0)
            take_x2(1, 0)
            take_y(0, 1)
            with dve.Fori(1, 3) as j:
                split_lo(p, j, 1)
                take_x2(j, 1)
                take_y(j, 0)
                split_lo(p, j + 1, 0)
                take_x2(j + 1, 0)
                take_y(j, 1)
            take_x2(3, 1)
            take_y(3, 0)
            take_y(3, 1)
            dve.wait_ge(ysums_turned, 1)
            sums = ps_main[:, 0, 0, :]
            dve.tensor_scalar(msq[:, 0:CH], sums[:, 0:CH], 1.0 / D, EPS, ALU.mult, ALU.add)
            dve.tensor_scalar(msq[0:NS, CH:CH + 1], sums[0:NS, CH:CH + 1], 1.0 / D, EPS,
                              ALU.mult, ALU.add).then_inc(msq_done, 1)
            inverse_root(5, last=rstd_ready)
            for c in range(CH + 1):
                if c not in ACT_Y:
                    n = ROWS[c]
                    dve.tensor_scalar(tok[0:n, c, :], tok[0:n, c, :], rstd[0:n, c:c + 1], None,
                                      ALU.mult).then_inc(y_ready, 1)

        @block.gpsimd
        def _(pool):
            pool.memset(sumsq[:], 1.0).then_inc(stats_set, 1)
            pool.memset(msq[:], 1.0).then_inc(stats_set, 1)
            pool.memset(root[:], 1.0).then_inc(stats_set, 1)
            pool.memset(rstd[:], 1.0).then_inc(stats_set, 1)
            pool.memset(ident[:], 0.0).then_inc(zero_set, 1)
            pool.memset(ones[:], 1.0).then_inc(consts_ready, 1)
            pool.wait_ge(zero_set, 1)
            pool.affine_select(out=ident[:], in_=ident[:], compare_op=ALU.not_equal, fill=1.0, base=0,
                               pattern=[[-1, P]], channel_multiplier=1).then_inc(consts_ready, 1)
            pool.memset(meanvar[:], 1.0).then_inc(pads_ready, 1)
            pool.memset(xc[:, 0:2], 0.0).then_inc(pads_ready, 1)

            pool.wait_ge(ws_copied, 1)
            pool.affine_select(out=ws_t[:], in_=ws_t[:], compare_op=ALU.is_ge, fill=0.0, base=0,
                               pattern=[[0, KD], [1, P]], channel_multiplier=-1).then_inc(ws_ready, 1)

            pool.wait_ge(ln_loaded, 32)
            for c in range(POOL_V):
                n = ROWS[c]
                pool.wait_ge(v_centred, c + 1)
                pool.tensor_tensor(tok[0:n, c, :], tok[0:n, c, :], lng_all[0:n, :], ALU.mult).then_inc(v_step, 1)
                pool.wait_ge(v_step, c + 1)
                pool.tensor_tensor(tok[0:n, c, :], tok[0:n, c, :], lnb_all[0:n, :], ALU.add).then_inc(v_ready, 1)

            def stage(g):
                pool.tensor_copy(v_stage[:, 0:CH, :], tok[:, 0:CH, bass.ds(P * g, P)])
                pool.tensor_copy(v_stage[0:NS, CH, :], tok[0:NS, CH, bass.ds(P * g, P)])
                pool.tensor_copy(ws_stage[:], ws_t[:, g, :]).then_inc(staged, 1)

            pool.wait_ge(v_ready, POOL_V)
            pool.wait_ge(v_ready_dve, CH + 1 - POOL_V)
            pool.wait_ge(ws_ready, 1)
            stage(0)
            with pool.Fori(1, KD) as g:
                pool.wait_ge(gated, g)
                pool.wait_ge(staged, g)
                stage(g)

            pool.wait_ge(a_ready, KD)
            pool.wait_ge(b_ready, KD)
            pool.tensor_tensor(resid[:], fbits(act_hi[:, XN:XN + KD, :]), fbits(act_lo[:, XN:XN + KD, :]),
                               ALU.add).then_inc(resid_ready, 1)

            p = ph["out"]
            pool.wait_ge(m_ready, 2 * KD)
            pool.memset(sq_sum[:], 0.0).then_inc(sum_done, 1)

            def add_square(j, s, i):
                m = 4 * j + 2 * s + i
                pool.wait_ge(dve_out[i], p.out_before(j, s, i) + 2)
                pool.wait_ge(sum_done, m + 1)
                pool.tensor_tensor(sq_one[:], resid[:, m, :], resid[:, m, :], ALU.mult).then_inc(sq_done, 1)
                pool.wait_ge(sq_done, m + 1)
                pool.tensor_tensor(sq_sum[:], sq_sum[:], sq_one[:], ALU.add).then_inc(sum_done, 1)

            with pool.Fori(0, 2) as j:
                for s in range(2):
                    for i in range(2):
                        add_square(j, s, i)

            pool.wait_ge(gate_out, KD)
            pool.memset(y_sum[:], 0.0).then_inc(ysum_done, 1)

            def add_y(m, slot):
                pool.wait_ge(ysq_done, m + 1)
                pool.wait_ge(ysum_done, m + 1)
                pool.tensor_tensor(y_sum[:], y_sum[:], y_sq[:, slot, :], ALU.add).then_inc(ysum_done, 1)

            with pool.Fori(0, 3) as j:
                add_y(2 * j, 0)
                add_y(2 * j + 1, 1)
            add_y(KD - 2, 0)


INS = ["x_prompt", "x_sample", "state_conv", "norm_mix", "w_in", "gmlp_ln_g", "gmlp_ln_b", "w_s", "b_s",
       "conv_w", "w_pa", "w_pb", "w_o", "norm_ffn", "w_gate", "w_up", "w_down", "norm_final"]


def kernel(**inputs):
    import numpy as _np
    import concourse.bacc as _bacc
    from concourse import mybir as _mybir
    from concourse.bass_utils import run_bass_kernel_spmd as _run

    nc = _bacc.Bacc("TRN2", target_bir_lowering=False, num_devices=1)
    arrays, args = {}, []
    for name in INS:
        a = _np.ascontiguousarray(inputs[name])
        arrays[f"in_{name}_dram"] = a
        args.append(nc.dram_tensor(f"in_{name}_dram", a.shape, _mybir.dt.from_np(a.dtype), kind="ExternalInput").ap())
    xp, xs, st = (inputs[n].shape for n in ("x_prompt", "x_sample", "state_conv"))
    outs = [xp, xs, (st[0], xp[0]) + tuple(st[2:]), st, (st[0],) + tuple(xs)]
    for i, shape in enumerate(outs):
        args.append(nc.dram_tensor(f"out_{i}_dram", tuple(shape), _mybir.dt.float32, kind="ExternalOutput").ap())
    trunk_kernel(nc, *args)
    r = _run(nc, [arrays], core_ids=[0])
    return tuple(r.results[0][f"out_{i}_dram"] for i in range(len(outs)))
```
